# Optimizing a Trainium2 kernel written in Bass

```python
import math
import jax, jax.numpy as jnp
from jax import lax
import numpy as np

D_MODEL = 2048
BATCH = 1
SEQ = 256
DEPTH = 2

CHUNK = 64
Q_BLOCK = 128

D_DIFF = D_MODEL // 2
DIFF_HEAD_DIM = 128
DIFF_QK_HALF = DIFF_HEAD_DIM // 2
N_DIFF_HEADS = D_DIFF // DIFF_HEAD_DIM
DIFF_SCALE = 1.0 / math.sqrt(DIFF_QK_HALF)

D_POOL = D_MODEL // 4
POOL_WINDOWS = (2, 4, 8, 16)
N_POOL_GROUPS = len(POOL_WINDOWS)
POOL_GROUP = D_POOL // N_POOL_GROUPS

CONV_CH = D_MODEL // 4
CONV_K = 31

D_IN = 3 * D_DIFF + D_POOL + 2 * CONV_CH
D_MIX = D_DIFF + D_POOL + CONV_CH

D_FF = ((8 * D_MODEL // 3 + 127) // 128) * 128
FFN_CONV_K = 3

RMS_EPS = 1e-6
LN_EPS = 1e-5

kernel_name = "hybrid_diffattn_pool_conformer_convffn"

def rmsnorm(x, g):
    xf = x.astype(jnp.float32)
    y = xf * lax.rsqrt(jnp.mean(xf * xf, axis=-1, keepdims=True) + RMS_EPS)
    return (y * g.astype(jnp.float32)).astype(x.dtype)

def layernorm(x, g, b):
    xf = x.astype(jnp.float32)
    mu = jnp.mean(xf, axis=-1, keepdims=True)
    var = jnp.mean(jnp.square(xf - mu), axis=-1, keepdims=True)
    y = (xf - mu) * lax.rsqrt(var + LN_EPS)
    return (y * g.astype(jnp.float32) + b.astype(jnp.float32)).astype(x.dtype)

def causal_dwconv(x, w, b):
    k = w.shape[0]
    y = lax.conv_general_dilated(
        x, w[:, None, :].astype(x.dtype), window_strides=(1,), padding=[(k - 1, 0)],
        dimension_numbers=("NWC", "WIO", "NWC"), feature_group_count=x.shape[-1])
    return y + b.astype(x.dtype)

def multiscale_pool(u, w_pool, pool_scale):
    bsz, s, _ = u.shape
    ug = u.reshape(bsz, s, N_POOL_GROUPS, POOL_GROUP)
    c = jnp.cumsum(ug.astype(jnp.float32), axis=1)
    t = jnp.arange(s)
    means = []
    for g, w in enumerate(POOL_WINDOWS):
        cg = c[:, :, g]
        lag = jnp.pad(cg, ((0, 0), (w, 0), (0, 0)))[:, :s]
        cnt = jnp.minimum(t + 1, w).astype(jnp.float32)[None, :, None]
        means.append((cg - lag) / cnt)
    pooled = jnp.stack(means, axis=2).astype(u.dtype) - ug
    y = jnp.einsum("bsgc,gcd->bsgd", pooled, w_pool)
    return y.reshape(bsz, s, D_POOL) * pool_scale

def diff_attention(q, k, v, lam, lam_init, head_gain):
    bsz, s, h, _ = q.shape
    nb = s // Q_BLOCK
    slopes = jnp.exp2(-8.0 * (jnp.arange(h, dtype=jnp.float32) + 1.0) / h)
    kpos = jnp.arange(s)
    k1, k2 = k[..., :DIFF_QK_HALF], k[..., DIFF_QK_HALF:]
    qb = q.reshape(bsz, nb, Q_BLOCK, h, 2 * DIFF_QK_HALF).transpose(1, 0, 2, 3, 4)

    def block(args):
        qblk, i = args
        tpos = i * Q_BLOCK + jnp.arange(Q_BLOCK)
        allowed = (kpos // CHUNK)[None, :] <= (tpos // CHUNK)[:, None]
        dist = jnp.abs(tpos[:, None] - kpos[None, :]).astype(jnp.float32)
        bias = jnp.where(allowed[None], -slopes[:, None, None] * dist[None], -jnp.inf)

        def probs(qh, kh):
            sc = jnp.einsum("bqhd,bkhd->bhqk", qh, kh).astype(jnp.float32) * DIFF_SCALE + bias
            return jax.nn.softmax(sc, axis=-1)

        a = probs(qblk[..., :DIFF_QK_HALF], k1) - lam * probs(qblk[..., DIFF_QK_HALF:], k2)
        return jnp.einsum("bhqk,bkhd->bqhd", a.astype(v.dtype), v)

    o = lax.map(block, (qb, jnp.arange(nb)))
    o = o.transpose(1, 0, 2, 3, 4).reshape(bsz, s, h, DIFF_HEAD_DIM)
    of = o.astype(jnp.float32)
    of = of * lax.rsqrt(jnp.mean(of * of, axis=-1, keepdims=True) + RMS_EPS)
    of = of * head_gain.astype(jnp.float32) * (1.0 - lam_init)
    return of.astype(v.dtype).reshape(bsz, s, h * DIFF_HEAD_DIM)

def conformer_conv(c_in, dw_w, dw_b, ln_g, ln_b, pw_w, pw_b):
    a = c_in[..., :CONV_CH] * jax.nn.sigmoid(c_in[..., CONV_CH:])
    a = causal_dwconv(a, dw_w, dw_b)
    a = jax.nn.silu(layernorm(a, ln_g, ln_b))
    return a @ pw_w + pw_b

def setup_inputs(seed: int = 0) -> dict:
    key = jax.random.key(seed)
    ks = jax.random.split(key, 24)
    f32 = jnp.float32
    nrm = lambda k, shape, scale: jax.random.normal(k, shape, f32) * scale
    L = DEPTH
    return {
        "x": jax.random.normal(ks[0], (BATCH, SEQ, D_MODEL), f32),
        "norm_mix": 1.0 + nrm(ks[1], (L, D_MODEL), 0.05),
        "w_in": nrm(ks[2], (L, D_MODEL, D_IN), D_MODEL ** -0.5),
        "lam_q1": nrm(ks[3], (L, DIFF_QK_HALF), 0.1),
        "lam_k1": nrm(ks[4], (L, DIFF_QK_HALF), 0.1),
        "lam_q2": nrm(ks[5], (L, DIFF_QK_HALF), 0.1),
        "lam_k2": nrm(ks[6], (L, DIFF_QK_HALF), 0.1),
        "diff_head_gain": 1.0 + nrm(ks[7], (L, N_DIFF_HEADS, DIFF_HEAD_DIM), 0.05),
        "pool_w": nrm(ks[8], (L, N_POOL_GROUPS, POOL_GROUP, POOL_GROUP), POOL_GROUP ** -0.5),
        "pool_scale": 1.0 + nrm(ks[9], (L, D_POOL), 0.1),
        "conv_dw_w": nrm(ks[10], (L, CONV_K, CONV_CH), CONV_K ** -0.5),
        "conv_dw_b": nrm(ks[11], (L, CONV_CH), 0.02),
        "conv_ln_g": 1.0 + nrm(ks[12], (L, CONV_CH), 0.05),
        "conv_ln_b": nrm(ks[13], (L, CONV_CH), 0.02),
        "conv_pw_w": nrm(ks[14], (L, CONV_CH, CONV_CH), CONV_CH ** -0.5),
        "conv_pw_b": nrm(ks[15], (L, CONV_CH), 0.02),
        "w_out": nrm(ks[16], (L, D_MIX, D_MODEL), D_MIX ** -0.5),
        "norm_ffn": 1.0 + nrm(ks[17], (L, D_MODEL), 0.05),
        "w_ffn_in": nrm(ks[18], (L, D_MODEL, 2 * D_FF), D_MODEL ** -0.5),
        "ffn_conv_w": nrm(ks[19], (L, FFN_CONV_K, D_FF), FFN_CONV_K ** -0.5),
        "ffn_conv_b": nrm(ks[20], (L, D_FF), 0.02),
        "w_ffn_out": nrm(ks[21], (L, D_FF, D_MODEL), D_FF ** -0.5),
        "final_norm": 1.0 + nrm(ks[22], (D_MODEL,), 0.05),
    }

def reference(x, norm_mix, w_in, lam_q1, lam_k1, lam_q2, lam_k2, diff_head_gain,
              pool_w, pool_scale, conv_dw_w, conv_dw_b, conv_ln_g, conv_ln_b,
              conv_pw_w, conv_pw_b, w_out, norm_ffn, w_ffn_in, ffn_conv_w,
              ffn_conv_b, w_ffn_out, final_norm):
    bsz, s, _ = x.shape
    o_k = D_DIFF
    o_v = 2 * D_DIFF
    o_a = 3 * D_DIFF
    o_c = 3 * D_DIFF + D_POOL
    for l in range(DEPTH):
        h = rmsnorm(x, norm_mix[l])
        p = h @ w_in[l]
        q = p[..., :o_k].reshape(bsz, s, N_DIFF_HEADS, DIFF_HEAD_DIM)
        k = p[..., o_k:o_v].reshape(bsz, s, N_DIFF_HEADS, DIFF_HEAD_DIM)
        v = p[..., o_v:o_a].reshape(bsz, s, N_DIFF_HEADS, DIFF_HEAD_DIM)
        a_in = p[..., o_a:o_c]
        c_in = p[..., o_c:]

        lam_init = 0.8 - 0.6 * math.exp(-0.3 * l)
        lam = (jnp.exp(jnp.sum(lam_q1[l].astype(jnp.float32) * lam_k1[l].astype(jnp.float32)))
               - jnp.exp(jnp.sum(lam_q2[l].astype(jnp.float32) * lam_k2[l].astype(jnp.float32)))
               + lam_init)
        y_b = diff_attention(q, k, v, lam, lam_init, diff_head_gain[l])
        y_a = multiscale_pool(a_in, pool_w[l], pool_scale[l])
        y_c = conformer_conv(c_in, conv_dw_w[l], conv_dw_b[l], conv_ln_g[l],
                             conv_ln_b[l], conv_pw_w[l], conv_pw_b[l])
        x = x + jnp.concatenate([y_b, y_a, y_c], axis=-1) @ w_out[l]

        h = rmsnorm(x, norm_ffn[l])
        gu = h @ w_ffn_in[l]
        g = causal_dwconv(gu[..., :D_FF], ffn_conv_w[l], ffn_conv_b[l])
        x = x + (jax.nn.silu(g) * gu[..., D_FF:]) @ w_ffn_out[l]
    return rmsnorm(x, final_norm)


_drawn_inputs = setup_inputs


def setup_inputs(seed=0):
    import zlib

    import numpy as np

    out = dict(_drawn_inputs(seed))
    spreads = {}
    factors = {'conv_dw_b': 3.396, 'conv_ln_b': 7.193, 'conv_pw_b': 4.502, 'ffn_conv_b': 4.652}
    for name, (base, spread) in spreads.items():
        noise = np.random.default_rng([zlib.crc32(name.encode()), seed]).standard_normal(out[name].shape)
        drawn = base * np.exp(spread * noise) if base else spread * noise
        out[name] = __import__('jax').numpy.asarray(drawn.astype(out[name].dtype))
    for name, factor in factors.items():
        out[name] = (out[name] * factor).astype(out[name].dtype)
    return out
```

```python
import math

LAYERS = 2
DM = 2048
S = 256
P = 128
KC = DM // P
NH = 8
HALF = 64
CHUNK = 64
FF = 5504
FC = FF // P
POOL_WINDOWS = (2, 4, 8, 16)
CONV_K = 31
PAD = CONV_K - 1
NT = 4
RING = 4
PB = 8
PIECE = PB * P

A_COLS = (3584, 4096, 2048, 0, 1024, 512, 1536, 2560, 3072)
CV, CG, V0, Q0, K0, Q1, K1, V1, PO = range(9)
A_TILES = (4, 4, 2, 4, 4, 4, 4, 2, 4)
B_CHUNKS = (12, 13, 14, 15, 0, 1, 2, 3, 8, 9, 10, 11, 4, 5, 6, 7)
CJ = FC // NT
CR = FC - CJ * NT
DP = (FC + 1) // 2

A0 = 0
B0 = A0 + 9 * 8
C0 = B0 + 4 * 8
CT = C0 + CJ * 16
D0 = CT + 12
PIECES = D0 + 4 * DP
assert PIECES % RING == 0
TA = [sum(A_TILES[:g]) for g in range(9)]
TB = sum(A_TILES)
TC = TB + 16
TT = TC + CJ * 8
TD = TT + 2 * NT
TILES = TD + 16
CREDIT = 8

P_NF, P_NN, P_HG, P_PS, P_DW = 0, 16, 32, 40, 44
P_DB = P_DW + 4 * CONV_K
P_LG, P_LB, P_PB = P_DB + 4, P_DB + 8, P_DB + 12
P_FF = P_DB + 16
NPAR = P_FF + 4 * FC
K_ND, K_ID, K_ON, K_IC = 0, 256, 384, 512
NCON = K_IC + 4 * 16

SCORE_AT = (42, 46, 50, 54, 59, 62, 65, 68)
LN_AT = 52


def group_ends():
    ends = [(g * 8 + 7, TA[g] + A_TILES[g] - 1) for g in range(9)]
    ends += [(B0 + 8 * g + 7, TB + 4 * g + 3) for g in range(4)]
    for j in range(CJ):
        ends += [(C0 + 16 * j + 7, TC + 8 * j + 3), (C0 + 16 * j + 15, TC + 8 * j + 7)]
    ends += [(CT + 5, TT + NT - 1), (CT + 11, TT + 2 * NT - 1)]
    ends += [(D0 + DP * g + DP - 1, TD + 4 * g + 3) for g in range(4)]
    return ends


ENDS = dict(group_ends())
SLOT_INCS = PIECES - len(ENDS)


def slot_count(idx):
    return idx + 1 - sum(1 for e in ENDS if e <= idx)


def lam_init(l):
    return 0.8 - 0.6 * math.exp(-0.3 * l)


STEPS = {"dve": 249, "loop": 5, "pool": 129}
SEEN = {}


def program(nc, xT, wstream, params, lamv, consts, poolw, pww, outT):
    import concourse.bass as bass
    from concourse import mybir
    from contextlib import ExitStack

    f32, f32r = mybir.dt.float32, mybir.dt.float32r
    ALU, ACT, AX = mybir.AluOpType, mybir.ActivationFunctionType, mybir.AxisListType

    ctx = ExitStack()
    with ctx:
        def sb(name, shape, dt=f32, where=ctx):
            return where.enter_context(nc.sbuf_tensor(name, shape, dt))

        def sem(name):
            return ctx.enter_context(nc.semaphore(name))

        x = sb("x", [P, KC, S])
        xg = sb("xg", [P, KC, 2 * S], f32r)
        raw = sb("raw", [P, RING, PIECE])
        whi = sb("whi", [P, RING, PIECE], f32r)
        wlo = sb("wlo", [P, RING, PIECE], f32r)
        con = sb("con", [P, NCON])
        par_all = sb("par_all", [P, LAYERS, NPAR + 1])
        par = sb("par", [P, NPAR + 1])
        gain0 = sb("gain0", [P, KC])
        credit = sb("credit", [P, 2])
        held = sb("held", [P, 2])
        eps = sb("eps", [P, 2])
        rstd = sb("rstd", [P, S + 2])
        ssq = sb("ssq", [P, S])
        sq = sb("sq", [P, 2, S])
        half = sb("half", [P, NT, S])
        gt = sb("gt", [P, NT, S + 2])
        y = sb("y", [P, NT, S])
        with ExitStack() as mixers:
            mix = sb("mix", [P, KC, 2 * S], f32r, mixers)
            qT = sb("qT", [P, NH, S], f32, mixers)
            kT = sb("kT", [P, NH, S], f32, mixers)
            v = sb("v", [P, 2, NH * P], f32, mixers)
            glu = sb("glu", [P, NT, PAD + S], f32, mixers)
            pw_sb = sb("pw_sb", [P, 4, 4 * P], f32, mixers)
            poolw_sb = sb("poolw_sb", [P, 4, P], f32, mixers)
            E = sb("E", [P, 2, 2, 3 * P], f32, mixers)
            att = sb("att", [P, 3 * P], f32, mixers)
            attT = sb("attT", [P, 3 * P], f32, mixers)
            bias = sb("bias", [P, 2, S], f32, mixers)
            junk = sb("junk", [P, 2, P], f32, mixers)
            mx = sb("mx", [P, NH, 4], f32, mixers)
            nmx = sb("nmx", [P, NH, 4], f32, mixers)
            sm = sb("sm", [P, NH, 4], f32, mixers)
            rs = sb("rs", [P, NH, 4], f32, mixers)
            hs = sb("hs", [P, NH, 2], f32, mixers)
            hr = sb("hr", [P, NH, 2], f32, mixers)
        hidden = sb("hidden", [P, FC, 2 * S], f32r)

        ps = [ctx.enter_context(nc.psum_tensor(f"bank{b}", [P, 512], f32)) for b in range(8)]
        S0, S1, AT = ps[4], ps[5], ps[6]
        OUT = AT[:, 0:S]
        MISC = ps[7][:, 0:S]
        POOLED = [ps[4][:, 0:S], ps[5][:, 0:S], MISC, ps[4][:, 0:S]]
        HEADS = [ps[6][:, 0:S], ps[5][:, 0:S], MISC, ps[4][:, 0:S]]
        negdist, ident, ones = con[:, K_ND:K_ND + S], con[:, K_ID:K_ID + P], con[:, K_ON:K_ON + P]

        raw_landed = [sem(f"raw_landed{s}") for s in range(RING)]
        hi_ready = sem("hi_ready")
        lo_ready = sem("lo_ready")
        slot_free = sem("slot_free")
        acc_done = sem("acc_done")
        evacuated = sem("evacuated")
        half_ready = sem("half_ready")
        xhi_ready = sem("xhi_ready")
        xg_ready = sem("xg_ready")
        ssq_ready = sem("ssq_ready")
        stat_done = sem("stat_done")
        rms_ready = sem("rms_ready")
        rstd_ready = sem("rstd_ready")
        params_ready = sem("params_ready")
        consts_loaded, gain_loaded = sem("consts_loaded"), sem("gain_loaded")
        params_loaded, lam_loaded = sem("params_loaded"), sem("lam_loaded")
        x_loaded = [sem(f"x_loaded{s}") for s in range(4)]
        smallw = [sem("pointwise_landed"), sem("poolw_landed")]
        setup_done = sem("setup_done")
        lam_exp = sem("lam_exp")
        gate_scaled = sem("gate_scaled")
        gated = sem("gated")
        glu_ready = sem("glu_ready")
        conv_done = sem("conv_done")
        pconv_done = sem("pconv_done")
        lnsum_done = sem("lnsum_done")
        mean_ready = sem("mean_ready")
        centred = sem("centred")
        squared = sem("squared")
        lnsq_done = sem("lnsq_done")
        lnstd_ready = sem("lnstd_ready")
        normed = sem("normed")
        swish_ready = sem("swish_ready")
        pw_done = sem("pw_done")
        chi_ready = sem("chi_ready")
        mixc_ready = sem("mixc_ready")
        qkv_ready = sem("qkv_ready")
        bias_ready = sem("bias_ready")
        scores_done = sem("scores_done")
        max_ready = sem("max_ready")
        exp_ready = sem("exp_ready")
        norms_ready = sem("norms_ready")
        first_map = sem("first_map")
        att_ready = sem("att_ready")
        attT_done = sem("attT_done")
        attT_ready = sem("attT_ready")
        head_done = sem("head_done")
        head_copied = sem("head_copied")
        head_sq = sem("head_sq")
        head_rms = sem("head_rms")
        head_scaled = sem("head_scaled")
        headT_done = sem("headT_done")
        hhi_ready = sem("hhi_ready")
        mixh_ready = sem("mixh_ready")
        pooled_ready = sem("pooled_ready")
        pool_done = sem("pool_done")
        phi_ready = sem("phi_ready")
        mixp_ready = sem("mixp_ready")
        gate_ready = sem("gate_ready")
        tap_ready = sem("tap_ready")
        taps_done = sem("taps_done")
        silu_ready = sem("silu_ready")
        hid_ready = sem("hid_ready")
        hidhi_ready = sem("hidhi_ready")
        hidden_ready = sem("hidden_ready")
        final_scaled = sem("final_scaled")
        dve_step = sem("dve_step")
        pool_step = sem("pool_step")
        stored = [sem(f"stored{q}") for q in range(4)]

        HALVES = 28 + 2 * FC
        HC = 28
        DVE_STEPS, DVE_LOOP = STEPS["dve"], STEPS["loop"]
        POOL_STEPS = STEPS["pool"]
        FFG = CJ + 1

        class Steps:

            def __init__(self, eng, s):
                self.eng, self.sem, self.base, self.n = eng, s, 0, 0

            def rebase(self, base):
                self.base, self.n = base, 0

            def step(self, ins):
                ins.then_inc(self.sem, 1)
                self.n += 1

            def settle(self, back=0):
                self.eng.wait_ge(self.sem, self.base + self.n - back)

        block = ctx.enter_context(nc.Block())

        @block.sync
        def _(sp):
            sp.dma_start(gain0[:], params[LAYERS][:, 0:KC]).then_inc(gain_loaded, 16)
            for s in range(RING):
                sp.dma_start(x[:, 4 * s:4 * s + 4, :], xT[:, 4 * s:4 * s + 4, :]).then_inc(x_loaded[s], 16)
                sp.dma_start(raw[:, s, :], wstream[s, :, :]).then_inc(raw_landed[s], 16)
            sp.dma_start(con[:], consts).then_inc(consts_loaded, 16)
            with sp.Fori(1, LAYERS * PIECES // RING + 1) as r:
                for s in range(RING):
                    sp.wait_ge(lo_ready, r * RING + (s - RING + 1))
                    sp.dma_start(raw[:, s, :], wstream[bass.ds(r * RING + s, 1), :, :]
                                 .rearrange("o p c -> p (o c)")).then_inc(raw_landed[s], 16)
            for q in range(4):
                sp.wait_ge(final_scaled, 4 * q + 4)
                sp.dma_start(outT[:, 4 * q:4 * q + 4, :], x[:, 4 * q:4 * q + 4, :]).then_inc(stored[q], 16)
            for q in range(4):
                sp.wait_ge(stored[q], 16)

        @block.scalar
        def _(act):
            for n, (dst, src) in enumerate(((par_all[:, :, 0:NPAR], params[0:LAYERS].rearrange("l p n -> p l n")),
                                            (y[:, 0:2, :].rearrange("p l n -> p (l n)"),
                                             lamv.partition_broadcast(P)))):
                act.dma_start(dst, src).then_inc((params_loaded, lam_loaded)[n], 16)
            act.wait_ge(gain_loaded, 16)
            for c in range(KC):
                if c % 4 == 0:
                    act.wait_ge(x_loaded[c // 4], 16)
                nc.scalar.activation(xg[:, c, 0:S], x[:, c, :], ACT.Copy,
                                     scale=gain0[:, c:c + 1]).then_inc(xhi_ready, 1)
                if c % 4 == 1:
                    s = c // 4
                    act.wait_ge(raw_landed[s], 16)
                    nc.scalar.activation(whi[:, s, :], raw[:, s, :], ACT.Copy).then_inc(hi_ready, 1)
            act.wait_ge(setup_done, 2)
            nc.scalar.activation(sm[:, 0, :], mx[:, 0, :], ACT.Exp).then_inc(lam_exp, 1)

            with act.Fori(0, LAYERS) as l:
                def hi(idx, rel, end_tile=None, count=None):
                    s = rel % RING
                    act.wait_ge(raw_landed[s], (l * (PIECES // RING) + (idx - s) // RING + 1) * 16
                                if isinstance(idx, int) else count[2])
                    if isinstance(idx, int):
                        old = idx - RING
                        if old in ENDS:
                            act.wait_ge(acc_done, l * TILES + ENDS[old] + 1)
                        else:
                            act.wait_ge(slot_free, l * SLOT_INCS + slot_count(old))
                    elif count[0] == "tile":
                        act.wait_ge(acc_done, count[1])
                    else:
                        act.wait_ge(slot_free, count[1])
                    nc.scalar.activation(whi[:, s, :], raw[:, s, :], ACT.Copy).then_inc(hi_ready, 1)

                def halves(tile, banks):
                    for i, b in enumerate(banks):
                        act.wait_ge(acc_done, l * TILES + tile + i + 1)
                        nc.scalar.activation(half[:, i, :], ps[b][:, S:2 * S], ACT.Copy).then_inc(half_ready, 1)

                def halves_a(g):
                    before = {CV: None, CG: TA[CG], Q0: None, K0: TA[K0], Q1: TA[Q1], K1: TA[K1], PO: TA[K1] + 4}[g]
                    if before:
                        act.wait_ge(evacuated, l * TILES + before + CREDIT)
                    if g == Q0:
                        act.wait_ge(glu_ready, l + 1)
                    halves(TA[g], range(NT))

                def residual_hi(g, tile, gains):
                    for i in range(NT):
                        c = 4 * g + i
                        act.wait_ge(evacuated, l * TILES + tile + i + 1 + CREDIT)
                        nc.scalar.activation(xg[:, c, 0:S], x[:, c, :], ACT.Copy,
                                             scale=par[:, gains + c:gains + c + 1]).then_inc(xhi_ready, 1)

                def rms(n):
                    act.wait_ge(stat_done, l * 2 + n + 1)
                    nc.scalar.activation(rstd[:], ps[4][:, 0:S + 2], ACT.Sqrt, bias=eps[:, 0:1],
                                         scale=1.0 / DM).then_inc(rms_ready, 1)

                hooks = {}

                def at(idx, fn, *args):
                    hooks.setdefault(idx, []).append((fn, args))

                def run(a, b):
                    for idx in range(a, b):
                        hi(idx, idx)
                        for fn, args in hooks.get(idx, ()):
                            fn(*args)

                def small_loads():
                    act.wait_ge(evacuated, l * TILES + CREDIT)
                    act.dma_start(pw_sb[:], pww[bass.ds(l, 1)].rearrange("o p c n -> p (o c) n")).then_inc(smallw[0], 16)
                    act.dma_start(poolw_sb[:], poolw[bass.ds(l, 1)].rearrange("o p c n -> p (o c) n")).then_inc(smallw[1], 16)

                def sigmoid():
                    act.wait_ge(gate_scaled, l + 1)
                    nc.scalar.activation(half[:], half[:], ACT.Sigmoid).then_inc(gated, 1)

                def ln_mean():
                    act.wait_ge(lnsum_done, l + 1)
                    nc.scalar.activation(y[:, 0, :], MISC, ACT.Copy, scale=1.0 / (4 * P)).then_inc(mean_ready, 1)

                def ln_square():
                    act.wait_ge(centred, l + 1)
                    nc.scalar.activation(y[:], gt[:, :, 0:S], ACT.Square).then_inc(squared, 1)

                def ln_std():
                    act.wait_ge(lnsq_done, l + 1)
                    nc.scalar.activation(y[:, 0, :], MISC, ACT.Sqrt, bias=eps[:, 1:2],
                                         scale=1.0 / (4 * P)).then_inc(lnstd_ready, 1)

                def swish():
                    act.wait_ge(normed, l + 1)
                    for i in range(4):
                        nc.scalar.activation(gt[:, i, 0:S], gt[:, i, 0:S], ACT.Silu, bias=par[:, P_LB + i:P_LB + i + 1],
                                             scale=par[:, P_LG + i:P_LG + i + 1]).then_inc(swish_ready, 1)

                def pw_hi(i):
                    act.wait_ge(pw_done, l * 4 + i + 1)
                    nc.scalar.activation(mix[:, 12 + i, 0:S], MISC, ACT.Identity,
                                         bias=par[:, P_PB + i:P_PB + i + 1]).then_inc(chi_ready, 1)

                def exps(h):
                    act.wait_ge(max_ready, l * NH + h + 1)
                    for b in range(2):
                        for m in range(2):
                            e = E[:, h % 2, m, b * P:P + 2 * P * b]
                            nc.scalar.activation(e, e, ACT.Exp, bias=nmx[:, h, 2 * b + m:2 * b + m + 1],
                                                 accum_out=sm[:, h, 2 * b + m:2 * b + m + 1]).then_inc(exp_ready, 1)

                def scale_first(h):
                    act.wait_ge(norms_ready, l * NH + h + 1)
                    if h:
                        act.wait_ge(attT_done, l * NH + h)
                    for b in range(2):
                        nc.scalar.activation(att[:, b * P:P + 2 * P * b], E[:, h % 2, 0, b * P:P + 2 * P * b], ACT.Copy,
                                             scale=rs[:, h, 2 * b:2 * b + 1]).then_inc(first_map, 1)

                def copy_attT(h):
                    act.wait_ge(attT_done, l * NH + h + 1)
                    if h:
                        act.wait_ge(head_done, l * NH + h)
                    nc.scalar.activation(attT[:], AT[:, 0:3 * P], ACT.Copy).then_inc(attT_ready, 1)

                def head_squares(h):
                    act.wait_ge(head_copied, l * NH + h + 1)
                    if h:
                        act.wait_ge(head_sq, l * 16 + 2 * h)
                    for b in range(2):
                        nc.scalar.activation(junk[:, b, :], OUT[:, b * P:b * P + P], ACT.Square,
                                             accum_out=hs[:, h, b:b + 1]).then_inc(head_sq, 1)

                def heads_rms(q):
                    act.wait_ge(head_sq, l * 16 + 8 * q + 8)
                    nc.scalar.activation(hr[:, 4 * q:4 * q + 4, :], hs[:, 4 * q:4 * q + 4, :], ACT.Sqrt,
                                         bias=eps[:, 0:1], scale=1.0 / P).then_inc(head_rms, 1)

                def head_hi(h, region):
                    act.wait_ge(headT_done, l * NH + h + 1)
                    nc.scalar.activation(mix[:, h, 0:S], region, ACT.Copy,
                                         scale=par[:, P_HG + h:P_HG + h + 1]).then_inc(hhi_ready, 1)

                def pool_hi(*tiles):
                    for i in tiles:
                        act.wait_ge(pool_done, l * 4 + i + 1)
                        nc.scalar.activation(mix[:, 8 + i, 0:S], POOLED[i], ACT.Copy,
                                             scale=par[:, P_PS + i:P_PS + i + 1]).then_inc(phi_ready, 1)

                def gate_halves(j, tile, nt):
                    if isinstance(j, int) and j == 0:
                        act.wait_ge(evacuated, l * TILES + TC + CREDIT)
                    else:
                        act.wait_ge(hidden_ready, l * FFG + j)
                    halves(tile, range(nt))

                def gate_taps(j, nt):
                    act.wait_ge(gate_ready, l * FFG + j + 1)
                    for i in range(nt):
                        col = P_FF + (j * NT + i) * 4
                        nc.scalar.activation(y[:, i, :], gt[:, i, 2:S + 2], ACT.Identity,
                                             bias=par[:, bass.ds(col + 3, 1)],
                                             scale=par[:, bass.ds(col + 2, 1)]).then_inc(tap_ready, 1)

                def gate_silu(j, nt):
                    act.wait_ge(taps_done, l * FC + j * NT + nt)
                    nc.scalar.activation(y[:, 0:nt, :], y[:, 0:nt, :], ACT.Silu).then_inc(silu_ready, 1)

                def up_halves(j, tile, nt):
                    act.wait_ge(evacuated, l * TILES + tile + CREDIT)
                    halves(tile, [4 + i for i in range(nt)])

                def hidden_hi(j, nt):
                    act.wait_ge(hid_ready, l * FFG + j + 1)
                    nc.scalar.activation(hidden[:, bass.ds(j * NT, nt), 0:S], half[:, 0:nt, :],
                                         ACT.Copy).then_inc(hidhi_ready, 1)

                at(RING, small_loads)
                at(8, rms, 0)
                for g in range(9):
                    if g not in (V0, V1):
                        at(8 * g + 10, halves_a, g)
                at(19, sigmoid)
                at(LN_AT + 3, ln_mean)
                at(LN_AT + 5, ln_square)
                at(LN_AT + 6, ln_std)
                at(LN_AT + 9, swish)
                for i in range(4):
                    at(LN_AT + 10 + i, pw_hi, i)
                for h in range(NH):
                    n = SCORE_AT[h]
                    at(n + 4, exps, h)
                    at(n + 6, scale_first, h)
                    at(n + 8, copy_attT, h)
                    at(n + 9, head_squares, h)
                at(64, heads_rms, 0)
                at(SCORE_AT[7] + 9, heads_rms, 1)
                for h in range(4):
                    at(67 + 2 * h, head_hi, h, MISC)
                    at(79 + h // 2, head_hi, 4 + h, HEADS[h])
                at(78, pool_hi, 0, 1, 2)
                at(79, pool_hi, 3)
                for g in range(4):
                    at(B0 + 8 * g + 10, residual_hi, g, TB + 4 * g, P_NF)
                at(C0 + 8, rms, 1)

                def pair_hooks(put, j, c, tile, ng, nt):
                    put(c + ng + 2, gate_halves, j, tile, nt)
                    put(c + ng + 3, gate_taps, j, nt)
                    put(c + ng + 5, gate_silu, j, nt)
                    put(c + 2 * ng + 2, up_halves, j, tile + NT, nt)
                    put(c + 2 * ng + 4, hidden_hi, j, nt)

                pair_hooks(at, 0, C0, TC, 8, NT)
                pair_hooks(at, CJ, CT, TT, 6, CR)
                for g in range(4):
                    if g < 3:
                        at(D0 + DP * (g + 1) + 2, residual_hi, g, TD + 4 * g, P_NN)
                run(RING, C0 + 21)
                with act.Fori(1, CJ) as j:
                    own = {}
                    pair_hooks(lambda k, *f: own.setdefault(k, []).append(f), j, 0, j * 8 + TC, 8, NT)
                    for rel in range(5, 21):
                        old = C0 + rel - RING
                        count = (("tile", l * TILES + j * 8 + ENDS[old] + 1) if old in ENDS else
                                 ("slot", l * SLOT_INCS + j * 14 + slot_count(old)))
                        s = (C0 + rel) % RING
                        landed = (l * (PIECES // RING) + j * 4 + (C0 + rel - s) // RING + 1) * 16
                        hi(j, C0 + rel, count=count + (landed,))
                        for f in own.get(rel, ()):
                            f[0](*f[1:])
                run(CT + 5, PIECES + 3)
                residual_hi(3, TD + 12, P_NN)
                run(PIECES + 3, PIECES + RING)

            act.wait_ge(stat_done, 2 * LAYERS + 1)
            nc.scalar.activation(rstd[:], ps[4][:, 0:S + 2], ACT.Sqrt, bias=eps[:, 0:1], scale=1.0 / DM).then_inc(rms_ready, 1)

        @block.vector
        def _(dve):
            st = Steps(dve, dve_step)
            step, settle = st.step, st.settle
            step(nc.vector.memset(eps[:, 0:1], 1e-6))
            step(nc.vector.memset(eps[:, 1:2], 1e-5))
            nc.vector.memset(credit[:, 1:2], 0.0).then_inc(evacuated, CREDIT)
            for c in range(KC):
                dve.wait_ge(xhi_ready, c + 1)
                nc.vector.scalar_tensor_tensor(out=xg[:, c, S:2 * S], in0=x[:, c, :], scalar=gain0[:, c:c + 1],
                                               in1=xg[:, c, 0:S], op0=ALU.mult, op1=ALU.subtract).then_inc(xg_ready, 1)
                if c % 4 == 1:
                    s = c // 4
                    dve.wait_ge(hi_ready, s + 1)
                    nc.vector.tensor_tensor(wlo[:, s, :], raw[:, s, :], whi[:, s, :], ALU.subtract).then_inc(lo_ready, 1)
            dve.wait_ge(lam_loaded, 16)
            for l in range(LAYERS):
                for m in range(2):
                    w = y[:, l, 128 * m:128 * m + 128]
                    step(nc.vector.tensor_tensor(y[:, 2 + l, 64 * m:64 * m + 64], w[:, 0:64], w[:, 64:128], ALU.mult))
            settle()
            for l in range(LAYERS):
                nc.vector.tensor_reduce(mx[:, 0, 2 * l:2 * l + 2], y[:, 2 + l, 0:128].rearrange("p (m d) -> p m d", m=2),
                                        AX.X, ALU.add).then_inc(setup_done, 1)
            dve.wait_ge(lam_exp, 1)
            dve.wait_ge(params_loaded, 16)
            for l in range(LAYERS):
                step(nc.vector.tensor_tensor(par_all[:, l, NPAR:NPAR + 1], sm[:, 0, 2 * l + 1:2 * l + 2],
                                             sm[:, 0, 2 * l:2 * l + 1], ALU.subtract))
                step(nc.vector.tensor_scalar(par_all[:, l, P_HG:P_HG + NH], par_all[:, l, P_HG:P_HG + NH],
                                             1.0 - lam_init(l), None, ALU.mult))
            settle()
            for l in range(LAYERS):
                step(nc.vector.tensor_scalar(par_all[:, l, NPAR:NPAR + 1], par_all[:, l, NPAR:NPAR + 1],
                                             -lam_init(l), None, ALU.add))
            settle()
            START = st.n

            with dve.Fori(0, LAYERS) as l:
                st.rebase(l * DVE_STEPS + START)

                def lo(idx, rel, landed=None):
                    s = rel % RING
                    dve.wait_ge(hi_ready, l * PIECES + idx + 1)
                    nc.vector.tensor_tensor(wlo[:, s, :], raw[:, s, :], whi[:, s, :], ALU.subtract).then_inc(lo_ready, 1)

                def add_halves(tile, banks, dst, h0):
                    for i, b in enumerate(banks):
                        dve.wait_ge(half_ready, l * HALVES + h0 + i + 1)
                        nc.vector.tensor_tensor(dst[i], ps[b][:, 0:S], half[:, i, :], ALU.add) \
                            .then_inc(evacuated, 1 if i < len(banks) - 1 else NT - i)
                    dve.wait_ge(evacuated, l * TILES + tile + NT + CREDIT)

                def rbc(nt):
                    return rstd[:, None, 0:S].to_broadcast([P, nt, S])

                H0 = {CV: 0, CG: 4, Q0: 8, K0: 12, Q1: 16, K1: 20, PO: 24}

                def evac_c(g):
                    dst = [glu[:, i, PAD:] for i in range(NT)] if g == CV else [half[:, i, :] for i in range(NT)]
                    if g == CV:
                        dve.wait_ge(acc_done, l * TILES + 1)
                        step(nc.vector.memset(glu[:, :, 0:PAD], 0.0))
                        dve.wait_ge(rstd_ready, l * 2 + 1)
                    add_halves(TA[g], range(NT), dst, H0[g])
                    if g == CV:
                        step(nc.vector.tensor_tensor(glu[:, :, PAD:], glu[:, :, PAD:], rbc(NT), ALU.mult))
                    else:
                        nc.vector.tensor_tensor(half[:], half[:], rbc(NT), ALU.mult).then_inc(gate_scaled, 1)

                def make_glu():
                    dve.wait_ge(gated, l + 1)
                    settle()
                    nc.vector.tensor_tensor(glu[:, :, PAD:], glu[:, :, PAD:], half[:], ALU.mult).then_inc(glu_ready, 1)

                taps = [(k, i) for k in range(CONV_K) for i in range(3)]

                def conv(a, b):
                    for n in range(a, min(b, len(taps))):
                        k, i = taps[n]
                        w = par[:, P_DW + i * CONV_K + k:P_DW + i * CONV_K + k + 1]
                        if k == 0:
                            if n == 0:
                                dve.wait_ge(glu_ready, l + 1)
                            step(nc.vector.tensor_scalar(gt[:, i, 0:S], glu[:, i, 0:S], w,
                                                         par[:, P_DB + i:P_DB + i + 1], ALU.mult, ALU.add))
                            continue
                        settle(2 - (i if k == CONV_K - 1 else 0))
                        ins = nc.vector.scalar_tensor_tensor(out=gt[:, i, 0:S], in0=glu[:, i, k:k + S], scalar=w,
                                                             in1=gt[:, i, 0:S], op0=ALU.mult, op1=ALU.add)
                        if k == CONV_K - 1:
                            ins.then_inc(conv_done, 1)
                        else:
                            step(ins)

                def ln_centre():
                    dve.wait_ge(mean_ready, l + 1)
                    nc.vector.tensor_tensor(gt[:, :, 0:S], gt[:, :, 0:S], y[:, 0:1, :].to_broadcast([P, NT, S]),
                                            ALU.subtract).then_inc(centred, 1)

                def ln_scale():
                    dve.wait_ge(lnstd_ready, l + 1)
                    step(nc.vector.reciprocal(y[:, 1, :], y[:, 0, :]))
                    settle()
                    nc.vector.tensor_tensor(gt[:, :, 0:S], gt[:, :, 0:S], y[:, 1:2, :].to_broadcast([P, NT, S]),
                                            ALU.mult).then_inc(normed, 1)

                def pw_lo(i):
                    dve.wait_ge(chi_ready, l * 4 + i + 1)
                    nc.vector.scalar_tensor_tensor(out=mix[:, 12 + i, S:2 * S], in0=MISC,
                                                   scalar=par[:, P_PB + i:P_PB + i + 1], in1=mix[:, 12 + i, 0:S],
                                                   op0=ALU.add, op1=ALU.subtract).then_inc(mixc_ready, 1)

                def evac_v(g):
                    hd = 0 if g == V0 else 4 * P
                    for t in range(2):
                        dve.wait_ge(acc_done, l * TILES + TA[g] + t + 1)
                        nc.vector.tensor_scalar(v[:, t, hd:hd + 4 * P], ps[t][:], rstd[:, S + t:S + t + 1], None,
                                                ALU.mult).then_inc(evacuated, 1)

                def evac_qk(g):
                    t, h = (qT, kT)[g in (K0, K1)], (0 if g in (Q0, K0) else 4)
                    add_halves(TA[g], range(NT), [t[:, h + i, :] for i in range(NT)], H0[g])
                    scale = HALF ** -0.5 if t is qT else 1.0
                    nc.vector.scalar_tensor_tensor(out=t[:, h:h + 4, :], in0=t[:, h:h + 4, :], scalar=scale,
                                                   in1=rbc(NT), op0=ALU.mult, op1=ALU.mult).then_inc(qkv_ready, 1)

                def maxes(h):
                    dve.wait_ge(bias_ready, l * NH + h + 1)
                    dve.wait_ge(scores_done, l * NH + h + 1)
                    step(nc.vector.memset(nmx[:, h, :], 0.0))
                    for b in range(2):
                        for m, bank in enumerate((S0, S1)):
                            sl = slice(b * P, P + 2 * P * b)
                            step(nc.vector.tensor_tensor_reduce(
                                out=E[:, h % 2, m, sl], in0=bank[:, sl], in1=bias[:, h % 2, P * (1 - b):S], scale=1.0,
                                scalar=-3.0e38, op0=ALU.add, op1=ALU.max, accum_out=mx[:, h, 2 * b + m:2 * b + m + 1]))
                    settle()
                    nc.vector.tensor_scalar(nmx[:, h, :], mx[:, h, :], -1.0, None, ALU.mult).then_inc(max_ready, 1)

                def inverse_sums(h):
                    dve.wait_ge(exp_ready, l * 32 + 4 * h + 4)
                    step(nc.vector.reciprocal(rs[:, h, :], sm[:, h, :]))
                    settle()
                    r2 = rs[:, h, :].rearrange("p (b m) -> p b m", m=2)[:, :, 1]
                    nc.vector.tensor_scalar(r2, r2, par[:, NPAR:NPAR + 1], None, ALU.mult).then_inc(norms_ready, 1)

                def combine(h):
                    for b in range(2):
                        dve.wait_ge(first_map, l * 16 + 2 * h + b + 1)
                        sl = slice(b * P, P + 2 * P * b)
                        nc.vector.scalar_tensor_tensor(out=att[:, sl], in0=E[:, h % 2, 1, sl],
                                                       scalar=rs[:, h, 2 * b + 1:2 * b + 2], in1=att[:, sl],
                                                       op0=ALU.mult, op1=ALU.add).then_inc(att_ready, 1)

                def copy_head(h):
                    dve.wait_ge(head_done, l * NH + h + 1)
                    nc.vector.tensor_copy(qT[:, h, :], OUT).then_inc(head_copied, 1)

                def scale_heads(q):
                    dve.wait_ge(head_rms, l * 2 + q + 1)
                    step(nc.vector.reciprocal(hr[:, 4 * q:4 * q + 4, :], hr[:, 4 * q:4 * q + 4, :]))
                    settle()
                    dve.wait_ge(head_copied, l * NH + 4 * q + 4)
                    for h in range(4 * q, 4 * q + 4):
                        for b in range(2):
                            o = qT[:, h, b * P:b * P + P]
                            nc.vector.tensor_scalar(o, o, hr[:, h, b:b + 1], None, ALU.mult).then_inc(head_scaled, 1)

                def head_lo(h, region):
                    dve.wait_ge(hhi_ready, l * NH + h + 1)
                    nc.vector.scalar_tensor_tensor(out=mix[:, h, S:2 * S], in0=region,
                                                   scalar=par[:, P_HG + h:P_HG + h + 1], in1=mix[:, h, 0:S],
                                                   op0=ALU.mult, op1=ALU.subtract).then_inc(mixh_ready, 1)

                def evac_pool():
                    add_halves(TA[PO], range(NT), [glu[:, i, PAD:] for i in range(NT)], H0[PO])
                    step(nc.vector.tensor_tensor(glu[:, :, PAD:], glu[:, :, PAD:], rbc(NT), ALU.mult))
                    settle()

                yf = y[:].rearrange("p a b -> p (a b)")
                W = PAD + S

                def pool_window(i, w):
                    if True:
                        src = glu[:, i, :]
                        first, shift = 0, 1
                        for r in range(i + 1):
                            dst = yf[:, (r % 2) * W:(r % 2) * W + W]
                            first += shift
                            step(nc.vector.tensor_tensor(dst[:, first:W], src[:, first:W],
                                                         src[:, first - shift:W - shift], ALU.add))
                            settle()
                            src, shift = dst, shift * 2
                        step(nc.vector.tensor_tensor(half[:, i, 0:16], src[:, PAD:PAD + 16],
                                                     con[:, K_IC + 16 * i:K_IC + 16 * i + 16], ALU.mult))
                        step(nc.vector.scalar_tensor_tensor(out=half[:, i, 16:S], in0=src[:, PAD + 16:W],
                                                            scalar=1.0 / w, in1=glu[:, i, PAD + 16:W],
                                                            op0=ALU.mult, op1=ALU.subtract))
                        settle()
                        nc.vector.tensor_tensor(half[:, i, 0:16], half[:, i, 0:16], glu[:, i, PAD:PAD + 16],
                                                ALU.subtract).then_inc(pooled_ready, 1)
                        settle()

                def pool_lo(*tiles):
                    for i in tiles:
                        dve.wait_ge(phi_ready, l * 4 + i + 1)
                        nc.vector.scalar_tensor_tensor(out=mix[:, 8 + i, S:2 * S], in0=POOLED[i],
                                                       scalar=par[:, P_PS + i:P_PS + i + 1], in1=mix[:, 8 + i, 0:S],
                                                       op0=ALU.mult, op1=ALU.subtract).then_inc(mixp_ready, 1)

                def copy_params():
                    dve.wait_ge(xg_ready, KC + l * 32)
                    nc.vector.tensor_copy(par[:], par_all[:, bass.ds(l, 1), :].rearrange("p o n -> p (o n)")) \
                        .then_inc(params_ready, 1)
                    dve.wait_ge(params_ready, l + 1)

                def inverse_rms(n):
                    dve.wait_ge(rms_ready, l * 2 + n + 1)
                    nc.vector.reciprocal(rstd[:], rstd[:]).then_inc(rstd_ready, 1)
                    dve.wait_ge(rstd_ready, l * 2 + n + 1)

                def residual(g, tile, first, gains, banks):
                    for i, b in enumerate(banks):
                        dve.wait_ge(acc_done, l * TILES + tile + i + 1)
                        step(nc.vector.tensor_tensor(half[:, i, :], ps[b][:, 0:S], x[:, 4 * g + i, :], ALU.add))
                    for i, b in enumerate(banks):
                        settle(3 - i)
                        nc.vector.tensor_tensor(x[:, 4 * g + i, :], ps[b][:, S:2 * S], half[:, i, :],
                                                ALU.add).then_inc(evacuated, 1)
                    for i, b in enumerate(banks):
                        c = 4 * g + i
                        dve.wait_ge(xhi_ready, KC + l * 32 + first + c + 1)
                        nc.vector.scalar_tensor_tensor(out=xg[:, c, S:2 * S], in0=x[:, c, :],
                                                       scalar=par[:, gains + c:gains + c + 1], in1=xg[:, c, 0:S],
                                                       op0=ALU.mult, op1=ALU.subtract).then_inc(xg_ready, 1)

                def gate_sums(j, tile, h0, nt):
                    add_halves(tile, range(nt), [gt[:, i, 2:] for i in range(nt)], h0)
                    nc.vector.tensor_tensor(gt[:, 0:nt, 2:], gt[:, 0:nt, 2:], rbc(nt), ALU.mult).then_inc(gate_ready, 1)

                def gate_taps(j, nt):
                    for k in (1, 0):
                        for i in range(nt):
                            col = P_FF + (j * NT + i) * 4 + k
                            if k:
                                dve.wait_ge(tap_ready, l * FC + j * NT + i + 1)
                            else:
                                settle(nt - 1 - i)
                            ins = nc.vector.scalar_tensor_tensor(out=y[:, i, :], in0=gt[:, i, k:k + S],
                                                                 scalar=par[:, bass.ds(col, 1)], in1=y[:, i, :],
                                                                 op0=ALU.mult, op1=ALU.add)
                            if k:
                                step(ins)
                            else:
                                ins.then_inc(taps_done, 1)

                def up_sums(j, tile, h0, nt):
                    add_halves(tile, [4 + i for i in range(nt)], [half[:, i, :] for i in range(nt)], h0)
                    step(nc.vector.tensor_tensor(half[:, 0:nt, :], half[:, 0:nt, :], rbc(nt), ALU.mult))

                def hidden_product(j, nt):
                    dve.wait_ge(silu_ready, l * FFG + j + 1)
                    settle()
                    nc.vector.tensor_tensor(half[:, 0:nt, :], half[:, 0:nt, :], y[:, 0:nt, :], ALU.mult) \
                        .then_inc(hid_ready, 1)

                def hidden_lo(j, nt):
                    dve.wait_ge(hidhi_ready, l * FFG + j + 1)
                    nc.vector.tensor_tensor(hidden[:, bass.ds(j * NT, nt), S:2 * S], half[:, 0:nt, :],
                                            hidden[:, bass.ds(j * NT, nt), 0:S], ALU.subtract).then_inc(hidden_ready, 1)

                def zero_front():
                    step(nc.vector.memset(gt[:, :, 0:2], 0.0))
                    settle()

                hooks = {}

                def at(idx, fn, *args):
                    hooks.setdefault(idx, []).append((fn, args))

                def run(a, b):
                    for idx in range(a, b):
                        lo(idx, idx)
                        for fn, args in hooks.get(idx, ()):
                            fn(*args)

                at(RING, copy_params)
                at(8, inverse_rms, 0)
                at(10, evac_c, CV)
                at(18, evac_c, CG)
                at(19, make_glu)
                for n in range(31):
                    at(20 + n, conv, 3 * n, 3 * n + 3)
                for g in (V0, V1):
                    at(8 * g + 10, evac_v, g)
                for g in (Q0, K0, Q1, K1):
                    at(8 * g + 10, evac_qk, g)
                at(LN_AT + 4, ln_centre)
                at(LN_AT + 8, ln_scale)
                for i in range(4):
                    at(LN_AT + 10 + i, pw_lo, i)
                at(74, evac_pool)
                for h in range(NH):
                    n = SCORE_AT[h]
                    at(n + 3, maxes, h)
                    at(n + 5, inverse_sums, h)
                    at(n + 6, combine, h)
                    at(n + 8, copy_head, h)
                at(65, scale_heads, 0)
                at(SCORE_AT[7] + 10, scale_heads, 1)
                for h in range(4):
                    at(68 + 2 * h, head_lo, h, MISC)
                    at(79 + h // 2, head_lo, 4 + h, HEADS[h])
                for i, w in enumerate(POOL_WINDOWS):
                    at((75, 75, 76, 77)[i], pool_window, i, w)
                at(78, pool_lo, 0, 1, 2)
                at(79, pool_lo, 3)
                for g in range(4):
                    at(B0 + 8 * g + 10, residual, g, TB + 4 * g, 0, P_NF, [4 * (g % 2) + i for i in range(NT)])
                at(C0 + 8, inverse_rms, 1)
                at(C0 + 9, zero_front)

                def pair_hooks(put, j, c, tile, ng, nt):
                    h0 = j * 8 + HC
                    put(c + ng + 2, gate_sums, j, tile, h0, nt)
                    put(c + ng + 4, gate_taps, j, nt)
                    put(c + 2 * ng + 2, up_sums, j, tile + NT, h0 + nt, nt)
                    put(c + 2 * ng + 3, hidden_product, j, nt)
                    put(c + 2 * ng + 4, hidden_lo, j, nt)

                pair_hooks(at, 0, C0, TC, 8, NT)
                pair_hooks(at, CJ, CT, TT, 6, CR)
                for g in range(3):
                    at(D0 + DP * (g + 1) + 2, residual, g, TD + 4 * g, 16, P_NN, [4 * (g % 2) + i for i in range(NT)])
                run(RING, C0 + 21)
                before = st.n
                with dve.Fori(1, CJ) as j:
                    st.rebase(l * DVE_STEPS + START + before + (j - 1) * DVE_LOOP)
                    own = {}
                    pair_hooks(lambda k, *f: own.setdefault(k, []).append(f), j, 0, j * 8 + TC, 8, NT)
                    for rel in range(5, 21):
                        lo(j * 16 + C0 + rel, C0 + rel)
                        for f in own.get(rel, ()):
                            f[0](*f[1:])
                SEEN["loop"] = st.n
                st.rebase(l * DVE_STEPS + START)
                st.n = before + (CJ - 1) * DVE_LOOP
                run(CT + 5, PIECES + 3)
                residual(3, TD + 12, 16, P_NN, [4 + i for i in range(NT)])
                run(PIECES + 3, PIECES + RING)
                SEEN["dve"] = st.n
            dve.wait_ge(rms_ready, 2 * LAYERS + 1)
            nc.vector.reciprocal(rstd[:], rstd[:]).then_inc(rstd_ready, 1)
            dve.wait_ge(rstd_ready, 2 * LAYERS + 1)
            for q in range(4):
                for i in range(NT):
                    c = 4 * q + i
                    nc.vector.scalar_tensor_tensor(out=x[:, c, :], in0=x[:, c, :],
                                                   scalar=par[:, P_NN + c:P_NN + c + 1], in1=rstd[:, 0:S],
                                                   op0=ALU.mult, op1=ALU.mult).then_inc(final_scaled, 1)

        @block.gpsimd
        def _(pool):
            st = Steps(pool, pool_step)
            step, settle = st.step, st.settle

            def hold_waits():
                settle()
                step(nc.gpsimd.tensor_tensor(held[:, 1:2], held[:, 0:1], held[:, 0:1], ALU.mult))

            step(nc.gpsimd.memset(held[:], 0.0))
            settle()

            def square_sum(wait):
                for c in range(KC):
                    wait(c)
                    dst = ssq[:] if c == 0 else sq[:, c % 2, :]
                    step(nc.gpsimd.tensor_tensor(dst, x[:, c, :], x[:, c, :], ALU.mult))
                    settle()
                    if 0 < c < KC - 1:
                        step(nc.gpsimd.tensor_tensor(ssq[:], ssq[:], sq[:, c % 2, :], ALU.add))
                        settle()
                    elif c:
                        nc.gpsimd.tensor_tensor(ssq[:], ssq[:], sq[:, c % 2, :], ALU.add).then_inc(ssq_ready, 1)

            def wait_load(c):
                if c % 4 == 0:
                    pool.wait_ge(x_loaded[c // 4], 16)

            square_sum(wait_load)
            pool.wait_ge(consts_loaded, 16)
            START = st.n
            with pool.Fori(0, LAYERS) as l:
                st.rebase(l * POOL_STEPS + START)

                def head_bias(h):
                    if h >= 2:
                        pool.wait_ge(max_ready, l * NH + h - 1)
                    else:
                        pool.wait_ge(acc_done, l * TILES + 1)
                    hold_waits()
                    nc.gpsimd.tensor_scalar(bias[:, h % 2, :], negdist, 2.0 ** (-8.0 * (h + 1) / NH), None,
                                            ALU.mult).then_inc(bias_ready, 1)

                head_bias(0)
                head_bias(1)
                i = 3
                pool.wait_ge(params_ready, l + 1)
                pool.wait_ge(glu_ready, l + 1)
                hold_waits()
                step(nc.gpsimd.tensor_scalar(gt[:, i, 0:S], glu[:, i, 0:S], par[:, P_DW + i * CONV_K:P_DW + i * CONV_K + 1],
                                             par[:, P_DB + i:P_DB + i + 1], ALU.mult, ALU.add))
                for k in range(1, CONV_K):
                    col = P_DW + i * CONV_K + k
                    step(nc.gpsimd.tensor_scalar(sq[:, k % 2, :], glu[:, i, k:k + S], par[:, col:col + 1], None, ALU.mult))
                    settle()
                    ins = nc.gpsimd.tensor_tensor(gt[:, i, 0:S], gt[:, i, 0:S], sq[:, k % 2, :], ALU.add)
                    if k < CONV_K - 1:
                        step(ins)
                    else:
                        ins.then_inc(pconv_done, 1)
                for h in range(2, NH):
                    head_bias(h)
                pool.wait_ge(pconv_done, l + 1)
                square_sum(lambda c: pool.wait_ge(evacuated, l * TILES + TB + c + 1 + CREDIT))
                pool.wait_ge(ssq_ready, l * 2 + 2)
                pool.wait_ge(stat_done, l * 2 + 2)
                square_sum(lambda c: pool.wait_ge(evacuated, l * TILES + TD + c + 1 + CREDIT))
                pool.wait_ge(ssq_ready, l * 2 + 3)
                SEEN["pool"] = st.n

        @block.tensor
        def _(pe):
            with pe.Fori(0, LAYERS) as l:
                def piece_mms(s, items, base):
                    pass

                def tile_block(bank, s, blk, mov, first, last):
                    nc.tensor.matmul(ps[bank][:], whi[:, s, blk * P:blk * P + P], mov, start=first, stop=False)
                    return nc.tensor.matmul(ps[bank][:, 0:S], wlo[:, s, blk * P:blk * P + P], mov[:, 0:S],
                                            start=False, stop=last)

                hooks = {}

                def at(idx, fn, *args):
                    hooks.setdefault(idx, []).append((fn, args))

                def arrived(idx, j=None):
                    pe.wait_ge(lo_ready, l * PIECES + idx + 1)

                def group(piece0, tile, free, banks, nk, moving, ready=None, rel0=None, hook=True):
                    nt = len(banks)
                    rel0 = piece0 if rel0 is None else rel0
                    per = PB if nt != NT else PB
                    blocks = [(k, i) for k in range(nk) for i in range(nt)]
                    npieces = -(-len(blocks) // PB)
                    for p in range(npieces):
                        s = (rel0 + p) % RING
                        arrived(piece0 + p)
                        mine = blocks[PB * p:PB * p + PB]
                        for blk, (k, i) in enumerate(mine):
                            if i == 0 and ready:
                                ready(k)
                            if k == 0:
                                pe.wait_ge(evacuated, l * TILES + free[i] + CREDIT)
                            last = tile_block(banks[i], s, blk, moving(k), k == 0, k == nk - 1)
                            if k == nk - 1:
                                last.then_inc(acc_done, 1 if i < nt - 1 else NT - i)
                            elif (k, i) == mine[-1]:
                                last.then_inc(slot_free, 1)
                        if hook:
                            for fn, args in hooks.get(piece0 + p, ()):
                                fn(*args)

                def v_group(piece0, tile, free):
                    for p in range(8):
                        s = (piece0 + p) % RING
                        arrived(piece0 + p)
                        for kk in range(2):
                            k = 2 * p + kk
                            for t in range(2):
                                if k == 0:
                                    pe.wait_ge(evacuated, l * TILES + free[t] + CREDIT)
                                xh = xg[:, k, t * P:t * P + P]
                                xl = xg[:, k, S + t * P:S + t * P + P]
                                wh = whi[:, s, kk * 512:kk * 512 + 512]
                                wl = wlo[:, s, kk * 512:kk * 512 + 512]
                                nc.tensor.matmul(ps[t][:], xh, wh, start=k == 0, stop=False)
                                nc.tensor.matmul(ps[t][:], xh, wl, start=False, stop=False)
                                last = nc.tensor.matmul(ps[t][:], xl, wh, start=False, stop=k == KC - 1)
                                if k == KC - 1:
                                    last.then_inc(acc_done, 1)
                                elif kk == 1 and t == 1:
                                    last.then_inc(slot_free, 1)
                        for fn, args in hooks.get(piece0 + p, ()):
                            fn(*args)

                def mm(out, lhsT, rhs, first=True, last=True):
                    return nc.tensor.matmul(out, lhsT, rhs, start=first, stop=last)

                def stats(n):
                    pe.wait_ge(consts_loaded, 16)
                    pe.wait_ge(ssq_ready, l * 2 + n + 1)
                    pe.wait_ge(evacuated, l * TILES + (TC if n else 0) + CREDIT)
                    mm(ps[4][:, 0:S], ones, ssq[:])
                    mm(ps[4][:, S:S + 1], ssq[:, 0:P], ones[:, 0:1])
                    mm(ps[4][:, S + 1:S + 2], ssq[:, P:S], ones[:, 0:1]).then_inc(stat_done, 1)

                def ln_sum():
                    pe.wait_ge(conv_done, l * 3 + 3)
                    pe.wait_ge(pconv_done, l + 1)
                    for i in range(4):
                        last = mm(MISC, ones, gt[:, i, 0:S], i == 0, i == 3)
                    last.then_inc(lnsum_done, 1)

                def ln_sq():
                    pe.wait_ge(squared, l + 1)
                    for i in range(4):
                        last = mm(MISC, ones, y[:, i, :], i == 0, i == 3)
                    last.then_inc(lnsq_done, 1)

                def pointwise(d):
                    if d == 0:
                        pe.wait_ge(smallw[0], (l + 1) * 16)
                        pe.wait_ge(swish_ready, l * 4 + 4)
                    else:
                        pe.wait_ge(mixc_ready, l * 4 + d)
                    for c in range(4):
                        last = mm(MISC, pw_sb[:, c, d * P:d * P + P], gt[:, c, 0:S], c == 0, c == 3)
                    last.then_inc(pw_done, 1)

                def scores(h):
                    pe.wait_ge(qkv_ready, l * 4 + (2 if h < 4 else 4))
                    if h == 0:
                        pe.wait_ge(rstd_ready, l * 2 + 1)
                    else:
                        pe.wait_ge(max_ready, l * NH + h)
                    for b in range(2):
                        for m, bank in enumerate((S0, S1)):
                            rows = slice(HALF * m, HALF * m + HALF)
                            last = mm(bank[:, b * P:P + 2 * P * b], qT[rows, h, b * P:b * P + P],
                                      kT[rows, h, 0:P * (b + 1)])
                    last.then_inc(scores_done, 1)

                def transpose_att(h):
                    pe.wait_ge(att_ready, l * 16 + 2 * h + 2)
                    if h:
                        pe.wait_ge(head_sq, l * 16 + 2 * h)
                    for n in range(3):
                        last = nc.tensor.transpose(AT[:, n * P:n * P + P], att[:, n * P:n * P + P], ident)
                    last.then_inc(attT_done, 1)

                def values(h):
                    pe.wait_ge(attT_ready, l * NH + h + 1)
                    if h in (0, 4):
                        pe.wait_ge(evacuated, l * TILES + TA[V0 if h == 0 else V1] + 2 + CREDIT)
                    hd = slice(h * P, h * P + P)
                    mm(OUT[:, 0:P], attT[:, 0:P], v[:, 0, hd])
                    mm(OUT[:, P:S], attT[:, P:2 * P], v[:, 0, hd], True, False)
                    mm(OUT[:, P:S], attT[:, 2 * P:3 * P], v[:, 1, hd], False, True).then_inc(head_done, 1)

                def transpose_head(h, region):
                    pe.wait_ge(head_scaled, l * 16 + 2 * h + 2)
                    if h == 0:
                        pe.wait_ge(mixc_ready, l * 4 + 4)
                    elif h < 4:
                        pe.wait_ge(mixh_ready, l * NH + h)
                    elif h > 4:
                        pe.wait_ge(mixp_ready, l * 4 + h - 3)
                    for b in range(2):
                        last = nc.tensor.transpose(region[:, b * P:b * P + P], qT[:, h, b * P:b * P + P], ident)
                    last.then_inc(headT_done, 1)

                def pool_products(*tiles):
                    pe.wait_ge(smallw[1], (l + 1) * 16)
                    for i in tiles:
                        pe.wait_ge(pooled_ready, l * 4 + i + 1)
                        if i == 0:
                            pe.wait_ge(max_ready, l * NH + NH)
                        elif i == 2:
                            pe.wait_ge(mixh_ready, l * NH + 4)
                        elif i == 3:
                            pe.wait_ge(mixp_ready, l * 4 + 1)
                        mm(POOLED[i], poolw_sb[:, i, :], half[:, i, :]).then_inc(pool_done, 1)

                at(5, stats, 0)
                at(LN_AT, ln_sum)
                at(LN_AT + 3, ln_sq)
                for i in range(4):
                    at(LN_AT + 6 + i, pointwise, i)
                for h in range(NH):
                    at(SCORE_AT[h] + 4, transpose_att, h)
                    at(SCORE_AT[h] + 5, values, h)
                for h in range(NH):
                    at(SCORE_AT[h], scores, h)
                at(75, pool_products, 0, 1, 2)
                at(76, pool_products, 3)
                for h in range(4):
                    at(64 + 2 * h, transpose_head, h, MISC)
                    at(76 + h // 2, transpose_head, 4 + h, HEADS[h])
                
                at(C0 + 5, stats, 1)

                def x_moving(k):
                    return xg[:, k, :]

                def x_from(n):
                    return lambda k: pe.wait_ge(xg_ready, l * 32 + 16 * n + k + 1)

                last_tile = {b: b - 8 + 1 for b in range(4)}
                for g in range(9):
                    free = [last_tile[i] for i in range(A_TILES[g])]
                    if g in (V0, V1):
                        v_group(8 * g, TA[g], free)
                    else:
                        group(8 * g, TA[g], free, range(4), KC, x_moving, x_from(0) if g == 0 else None)
                    for i in range(A_TILES[g]):
                        last_tile[i] = TA[g] + i + 1

                def mix_ready(k):
                    c = B_CHUNKS[k]
                    if c >= 12:
                        pe.wait_ge(mixc_ready, l * 4 + c - 12 + 1)
                    elif c < 8:
                        pe.wait_ge(mixh_ready, l * NH + c + 1)
                    else:
                        pe.wait_ge(mixp_ready, l * 4 + c - 8 + 1)

                for g in range(4):
                    tile = TB + 4 * g
                    free = [TA[PO] + i + 1 if g == 0 else 0 if g == 1 else tile + i + 1 - 8 for i in range(4)]
                    group(B0 + 8 * g, tile, free, [4 * (g % 2) + i for i in range(4)], KC,
                          lambda k: mix[:, B_CHUNKS[k], :], mix_ready if g == 0 else None)

                group(C0, TC, [TC + i + 1 - 8 for i in range(4)], range(4), KC, x_moving,
                      x_from(1))
                pe.wait_ge(rstd_ready, l * 2 + 2)
                group(C0 + 8, TC + 4, [TC + 4 + i + 1 - 8 for i in range(4)], range(4, 8), KC, x_moving)
                with pe.Fori(1, CJ) as j:
                    for u in range(2):
                        tile = TC + 4 * u
                        group(j * 16 + C0 + 8 * u, 0, [j * 8 + (tile + i + 1 - 8) for i in range(4)],
                              range(4 * u, 4 * u + 4), KC, x_moving, rel0=C0 + 8 * u, hook=False)
                for u in range(2):
                    group(CT + 6 * u, 0, [TT - 8 + 4 * u + i + 1 for i in range(CR)], range(4 * u, 4 * u + CR),
                          KC, x_moving)

                with pe.Fori(0, 2) as d:
                    for u in range(2):
                        tile = TD + 4 * u
                        group(d * (2 * DP) + D0 + DP * u, 0, [d * 8 + (tile + i + 1 - 8) for i in range(4)],
                              range(4 * u, 4 * u + 4), FC, lambda k: hidden[:, k, :],
                              (lambda k: pe.wait_ge(hidden_ready, l * FFG + k // NT + 1) if k % NT == 0 else None)
                              if u == 0 else None, rel0=D0 + DP * u, hook=False)
            pe.wait_ge(ssq_ready, 2 * LAYERS + 1)
            pe.wait_ge(evacuated, LAYERS * TILES + CREDIT)
            mm(ps[4][:, 0:S], ones, ssq[:])
            mm(ps[4][:, S:S + 1], ssq[:, 0:P], ones[:, 0:1])
            mm(ps[4][:, S + 1:S + 2], ssq[:, P:S], ones[:, 0:1]).then_inc(stat_done, 1)

    assert SEEN == STEPS, SEEN


def lay_out(a):
    import numpy as np
    f = np.float32
    xT = np.ascontiguousarray(a["x"][0].T.reshape(KC, P, S).transpose(1, 0, 2))

    def blocks(w, cols, chunks):
        nt = cols[1] // P
        n = len(chunks) * nt
        out = np.zeros((-(-n // PB), PB, P, P), f)
        b = w.reshape(-1, P, w.shape[1])[chunks][:, :, cols[0]:cols[0] + cols[1]]
        out.reshape(-1, P, P)[:n] = b.reshape(len(chunks), P, nt, P).transpose(0, 2, 1, 3).reshape(n, P, P)
        return out.transpose(0, 2, 1, 3).reshape(-1, P, PIECE)

    stream = []
    for l in range(LAYERS):
        every = list(range(KC))
        for c in A_COLS:
            stream.append(blocks(a["w_in"][l], (c, 512), every))
        for g in range(4):
            stream.append(blocks(a["w_out"][l], (512 * g, 512), list(B_CHUNKS)))
        for j in range(CJ + 1):
            n = 512 if j < CJ else CR * P
            for u in range(2):
                stream.append(blocks(a["w_ffn_in"][l], (u * FF + 512 * j, n), every))
        for g in range(4):
            stream.append(blocks(a["w_ffn_out"][l], (512 * g, 512), list(range(FC))))
    stream.append(np.zeros((RING, P, PIECE), f))
    wstream = np.concatenate(stream)

    def col(v):
        return v.reshape(-1, P).T

    params = np.zeros((LAYERS + 1, P, NPAR), f)
    for l in range(LAYERS):
        q = params[l]
        q[:, P_NF:P_NF + KC] = col(a["norm_ffn"][l])
        q[:, P_NN:P_NN + KC] = col(a["norm_mix"][l + 1] if l + 1 < LAYERS else a["final_norm"])
        q[:, P_HG:P_HG + NH] = a["diff_head_gain"][l].T
        q[:, P_PS:P_PS + 4] = col(a["pool_scale"][l])
        q[:, P_DW:P_DB] = a["conv_dw_w"][l].T.reshape(4, P, CONV_K).transpose(1, 0, 2).reshape(P, -1)
        q[:, P_DB:P_DB + 4] = col(a["conv_dw_b"][l])
        q[:, P_LG:P_LG + 4] = col(a["conv_ln_g"][l])
        q[:, P_LB:P_LB + 4] = col(a["conv_ln_b"][l])
        q[:, P_PB:P_PB + 4] = col(a["conv_pw_b"][l])
        ff = np.concatenate([a["ffn_conv_w"][l], a["ffn_conv_b"][l][None]])
        q[:, P_FF:] = ff.T.reshape(FC, P, 4).transpose(1, 0, 2).reshape(P, -1)
    params[LAYERS, :, 0:KC] = col(a["norm_mix"][0])
    lamv = np.stack([a["lam_q1"], a["lam_k1"], a["lam_q2"], a["lam_k2"]], 1).reshape(1, -1)

    consts = np.zeros((P, NCON), f)
    q, k = P + np.arange(P)[:, None], np.arange(S)[None]
    consts[:, K_ND:K_ND + S] = np.where(k // CHUNK <= q // CHUNK, -np.abs(q - k), -1e30)
    consts[:, K_ID:K_ID + P] = np.eye(P)
    consts[:, K_ON:K_ON + P] = 1
    for i, w in enumerate(POOL_WINDOWS):
        consts[:, K_IC + 16 * i:K_IC + 16 * i + 16] = 1.0 / np.minimum(np.arange(16) + 1, w)
    poolw = np.ascontiguousarray(a["pool_w"].transpose(0, 2, 1, 3))
    pww = np.ascontiguousarray(a["conv_pw_w"].reshape(LAYERS, 4, P, 4 * P).transpose(0, 2, 1, 3))
    return dict(xT=xT, wstream=wstream, params=params, lamv=np.ascontiguousarray(lamv), consts=consts,
                poolw=poolw, pww=pww)


def kernel(**inputs):
    import numpy as np
    import concourse.bacc as bacc
    from concourse import mybir
    from concourse.bass_utils import run_bass_kernel_spmd

    arrays = lay_out({n: np.asarray(v) for n, v in inputs.items()})
    nc = bacc.Bacc("TRN2", target_bir_lowering=False, num_devices=1)
    aps = [nc.dram_tensor(n, v.shape, mybir.dt.from_np(v.dtype), kind="ExternalInput").ap() for n, v in arrays.items()]
    outT = nc.dram_tensor("outT", (P, KC, S), mybir.dt.float32, kind="ExternalOutput").ap()
    program(nc, *aps, outT)
    got = run_bass_kernel_spmd(nc, [arrays], core_ids=[0]).results[0]["outT"]
    return np.ascontiguousarray(got.transpose(2, 1, 0).reshape(1, S, DM))
```

```python
import math

LAYERS = 2
DM = 2048
S = 256
P = 128
KC = DM // P
NH = 8
HALF = 64
CHUNK = 64
FF = 5504
FC = FF // P
POOL_WINDOWS = (2, 4, 8, 16)
CONV_K = 31
PAD = CONV_K - 1
NT = 4
RING = 4
PB = 8
PIECE = PB * P

A_COLS = (3584, 4096, 2048, 0, 1024, 512, 1536, 2560, 3072)
CV, CG, V0, Q0, K0, Q1, K1, V1, PO = range(9)
A_TILES = (4, 4, 2, 4, 4, 4, 4, 2, 4)
A_BANKS = ((0, 1, 2, 3), (0, 1, 2, 3), (0, 1)) + ((2, 3, 0, 1),) * 4 + ((2, 3), (0, 1, 2, 3))
B_CHUNKS = (12, 13, 14, 15, 0, 1, 2, 3, 8, 9, 10, 11, 4, 5, 6, 7)
CJ = FC // NT
CR = FC - CJ * NT
DP = (FC + 1) // 2

A0 = 0
B0 = A0 + 9 * 8
C0 = B0 + 4 * 8
CT = C0 + CJ * 16
D0 = CT + 12
PIECES = D0 + 4 * DP
assert PIECES % RING == 0
TA = [sum(A_TILES[:g]) for g in range(9)]
TB = sum(A_TILES)
TC = TB + 16
TT = TC + CJ * 8
TD = TT + 2 * NT
TILES = TD + 16
CREDIT = 8

P_NF, P_NN, P_HG, P_PS, P_DW = 0, 16, 32, 40, 44
P_DB = P_DW + 4 * CONV_K
P_LG, P_LB, P_PB = P_DB + 4, P_DB + 8, P_DB + 12
P_FF = P_DB + 16
P_LI = P_FF + 4 * FC
NPAR = P_LI + 2
P_LAM = NPAR
K_ND, K_ID, K_ON, K_IC = 0, 256, 384, 512
NCON = K_IC + 4 * 16

SCORE_AT = (41, 44, 47, 50, 57, 60, 62, 65)
VALUES_AT = (47, 50, 53, 56, 64, 66, 68, 71)
LN_AT = 49
POOL_CHUNKS = 4
STORES = ((4, 2), (6, 2), (8, 2), (10, 2), (0, 4), (12, 2), (14, 2))
FIRST_X = 8
X_LOADS = {0: 0, 2: 1, 4: 2, 8: 3, 12: 4}


def group_ends():
    ends = [(g * 8 + 7, TA[g] + A_TILES[g] - 1) for g in range(9)]
    ends += [(B0 + 8 * g + 7, TB + 4 * g + 3) for g in range(4)]
    for j in range(CJ):
        ends += [(C0 + 16 * j + 7, TC + 8 * j + 3), (C0 + 16 * j + 15, TC + 8 * j + 7)]
    ends += [(CT + 5, TT + NT - 1), (CT + 11, TT + 2 * NT - 1)]
    ends += [(D0 + DP * g + DP - 1, TD + 4 * g + 3) for g in range(4)]
    return ends


ENDS = dict(group_ends())
SLOT_INCS = PIECES - len(ENDS)


def slot_count(idx):
    return idx + 1 - sum(1 for e in ENDS if e <= idx)


def lam_init(l):
    return 0.8 - 0.6 * math.exp(-0.3 * l)


STEPS = {"dve": 211, "loop": 5, "pool": 128}
SEEN = {}


def program(nc, xT, wstream, params, lamv, consts, poolw, pww, outT):
    import concourse.bass as bass
    from concourse import mybir
    from contextlib import ExitStack

    f32, f32r = mybir.dt.float32, mybir.dt.float32r
    ALU, ACT, AX = mybir.AluOpType, mybir.ActivationFunctionType, mybir.AxisListType

    ctx = ExitStack()
    with ctx:
        def sb(name, shape, dt=f32, where=ctx):
            return where.enter_context(nc.sbuf_tensor(name, shape, dt))

        def sem(name):
            return ctx.enter_context(nc.semaphore(name))

        x = sb("x", [P, KC, S])
        xg = sb("xg", [P, KC, 2 * S], f32r)
        raw = sb("raw", [P, RING, PIECE])
        whi = sb("whi", [P, RING, PIECE], f32r)
        wlo = sb("wlo", [P, RING, PIECE], f32r)
        con = sb("con", [P, NCON])
        par = sb("par", [P, NPAR + 1])
        credit = sb("credit", [P, 2])
        held = sb("held", [P, 2])
        eps = sb("eps", [P, 2])
        rstd = sb("rstd", [P, S + 2])
        ssq = sb("ssq", [P, S])
        win1 = sb("win1", [P, 2, PAD + S])
        sq = sb("sq", [P, 2, S])
        half = sb("half", [P, NT, S])
        gt = sb("gt", [P, NT, S + 2])
        y = sb("y", [P, NT, S])
        with ExitStack() as mixers:
            mix = sb("mix", [P, KC, 2 * S], f32r, mixers)
            qT = sb("qT", [P, NH, S], f32, mixers)
            kT = sb("kT", [P, NH, S], f32, mixers)
            v = sb("v", [P, 2, NH * P], f32, mixers)
            glu = sb("glu", [P, NT, PAD + S], f32, mixers)
            pw_sb = sb("pw_sb", [P, 4, 4 * P], f32, mixers)
            poolw_sb = sb("poolw_sb", [P, 4, P], f32, mixers)
            E = sb("E", [P, 2, 2, 3 * P], f32, mixers)
            att = sb("att", [P, 3 * P], f32, mixers)
            attT = sb("attT", [P, 3 * P], f32, mixers)
            bias = sb("bias", [P, 2, S], f32, mixers)
            junk = sb("junk", [P, 2, P], f32, mixers)
            win0 = sb("win0", [P, 2, PAD + S], f32, mixers)
            mx = sb("mx", [P, NH, 4], f32, mixers)
            nmx = sb("nmx", [P, NH, 4], f32, mixers)
            sm = sb("sm", [P, NH, 4], f32, mixers)
            rs = sb("rs", [P, NH, 4], f32, mixers)
            hs = sb("hs", [P, NH, 2], f32, mixers)
            hr = sb("hr", [P, NH, 2], f32, mixers)
        hidden = sb("hidden", [P, FC, 2 * S], f32r)

        ps = [ctx.enter_context(nc.psum_tensor(f"bank{b}", [P, 512], f32)) for b in range(8)]
        S0, S1, AT = ps[4], ps[5], ps[6]
        OUT = AT[:, 0:S]
        MISC = ps[7][:, 0:S]
        POOLED = [ps[4][:, 0:S], ps[5][:, 0:S], MISC, ps[6][:, 0:S]]
        HEADS = POOLED
        lam_all = E[:, 0].rearrange("p m k -> p (m k)")
        lam_in, lam_prod = lam_all[:, 0:256], lam_all[:, 256:384]
        negdist, ident, ones = con[:, K_ND:K_ND + S], con[:, K_ID:K_ID + P], con[:, K_ON:K_ON + P]

        raw_landed = [sem(f"raw_landed{s}") for s in range(RING)]
        hi_ready = sem("hi_ready")
        lo_ready = sem("lo_ready")
        slot_free = sem("slot_free")
        acc_done = sem("acc_done")
        evacuated = sem("evacuated")
        half_ready = sem("half_ready")
        xhi_ready = sem("xhi_ready")
        xg_ready = sem("xg_ready")
        ssq_ready = sem("ssq_ready")
        ssq_part = sem("ssq_part")
        end_squared = sem("end_squared")
        windowed = sem("windowed")
        stat_done = sem("stat_done")
        rms_ready = sem("rms_ready")
        rstd_ready = sem("rstd_ready")
        params_loaded = sem("params_loaded")
        half_landed, half_hi = sem("half_landed"), sem("half_hi")
        lam_loaded = sem("lam_loaded")
        lam_dots = sem("lam_dots")
        lam_exp = sem("lam_exp")
        consts_loaded, gain_loaded = sem("consts_loaded"), sem("gain_loaded")
        x_loaded = [sem(f"x_loaded{s}") for s in range(5)]
        pointwise_landed, poolw_landed = sem("pointwise_landed"), sem("poolw_landed")
        gate_scaled = sem("gate_scaled")
        gated = sem("gated")
        glu_ready = sem("glu_ready")
        conv_done = sem("conv_done")
        pconv_done = sem("pconv_done")
        presummed = sem("presummed")
        lnsum_done = sem("lnsum_done")
        mean_ready = sem("mean_ready")
        centred = sem("centred")
        squared = sem("squared")
        lnsq_done = sem("lnsq_done")
        lnstd_ready = sem("lnstd_ready")
        normed = sem("normed")
        swish_ready = sem("swish_ready")
        pw_done = sem("pw_done")
        chi_ready = sem("chi_ready")
        mixc_ready = sem("mixc_ready")
        qkv_ready = sem("qkv_ready")
        bias_ready = sem("bias_ready")
        scores_done = sem("scores_done")
        max_ready = sem("max_ready")
        exp_ready = sem("exp_ready")
        norms_ready = sem("norms_ready")
        first_map = sem("first_map")
        att_ready = sem("att_ready")
        attT_done = sem("attT_done")
        attT_ready = sem("attT_ready")
        head_done = sem("head_done")
        head_copied = sem("head_copied")
        head_sq = sem("head_sq")
        head_rms = sem("head_rms")
        head_scaled = sem("head_scaled")
        headT_done = sem("headT_done")
        hhi_ready = sem("hhi_ready")
        mixh_ready = sem("mixh_ready")
        pool_in = sem("pool_in")
        pooled_ready = sem("pooled_ready")
        pool_done = sem("pool_done")
        phi_ready = sem("phi_ready")
        mixp_ready = sem("mixp_ready")
        gate_ready = sem("gate_ready")
        tap_ready = sem("tap_ready")
        taps_done = sem("taps_done")
        silu_ready = sem("silu_ready")
        hid_ready = sem("hid_ready")
        hidhi_ready = sem("hidhi_ready")
        hidden_ready = sem("hidden_ready")
        prescaled = sem("prescaled")
        final_scaled, pool_scaled = sem("final_scaled"), sem("pool_scaled")
        dve_step = sem("dve_step")
        pool_step = sem("pool_step")
        stored = [sem(f"stored{q}") for q in range(7)]

        HALVES = 28 + 2 * FC
        HC = 28
        DVE_STEPS, DVE_LOOP = STEPS["dve"], STEPS["loop"]
        POOL_STEPS = STEPS["pool"]
        FFG = CJ + 1

        class Steps:

            def __init__(self, eng, s):
                self.eng, self.sem, self.base, self.n = eng, s, 0, 0

            def rebase(self, base):
                self.base, self.n = base, 0

            def step(self, ins):
                ins.then_inc(self.sem, 1)
                self.n += 1

            def settle(self, back=0):
                self.eng.wait_ge(self.sem, self.base + self.n - back)

        block = ctx.enter_context(nc.Block())

        @block.sync
        def _(sp):
            sp.dma_start(par[:, P_NN:P_NN + KC], params[LAYERS][:, 0:KC]).then_inc(gain_loaded, 16)
            first_loads = ((0, 2), (2, 2), (4, 4))
            for s, (c, n) in enumerate(first_loads):
                sp.dma_start(x[:, c:c + n, :], xT[:, c:c + n, :]).then_inc(x_loaded[s], 16)
                if s == 0:
                    sp.dma_start(raw[:, 0, 0:PIECE // 2], wstream[0, :, 0:PIECE // 2]).then_inc(half_landed, 16)
                    sp.dma_start(raw[:, 0, PIECE // 2:], wstream[0, :, PIECE // 2:]).then_inc(raw_landed[0], 16)
                else:
                    sp.dma_start(raw[:, s, :], wstream[s, :, :]).then_inc(raw_landed[s], 16)
            sp.dma_start(raw[:, 3, :], wstream[3, :, :]).then_inc(raw_landed[3], 16)
            for s, c in ((3, 8), (4, 12)):
                sp.dma_start(x[:, c:c + 4, :], xT[:, c:c + 4, :]).then_inc(x_loaded[s], 16)

            def load(r, s):
                sp.wait_ge(lo_ready, r * RING + (s - RING + 1))
                sp.dma_start(raw[:, s, :], wstream[bass.ds(r * RING + s, 1), :, :]
                             .rearrange("o p c -> p (o c)")).then_inc(raw_landed[s], 16)

            with sp.Fori(1, LAYERS * PIECES // RING) as r:
                for s in range(RING):
                    load(r, s)
            for s in range(2):
                load(LAYERS * PIECES // RING, s)
            for q, (c, n) in enumerate(STORES):
                if c:
                    sp.wait_ge(final_scaled, c + n - POOL_CHUNKS)
                else:
                    sp.wait_ge(pool_scaled, 1)
                sp.dma_start(outT[:, c:c + n, :], x[:, c:c + n, :]).then_inc(stored[q], 16)
            for q in range(len(STORES)):
                sp.wait_ge(stored[q], 16)

        @block.scalar
        def _(act):
            def gain_hi(c, gains):
                nc.scalar.activation(xg[:, c, 0:S], x[:, c, :], ACT.Copy,
                                     scale=par[:, gains + c:gains + c + 1]).then_inc(xhi_ready, 1)

            def square(i):
                nc.scalar.activation(y[:, i, :], x[:, 12 + i, :], ACT.Square).then_inc(end_squared, 1)

            act.wait_ge(gain_loaded, 16)
            nc.scalar.activation(credit[:, 0:1], par[:, P_NN:P_NN + 1], ACT.Copy)
            for c in range(FIRST_X):
                if c in X_LOADS:
                    act.wait_ge(x_loaded[X_LOADS[c]], 16)
                gain_hi(c, P_NN)
                if c in (1, 3):
                    s, first = c // 2, 0
                    if s == 0:
                        first = PIECE // 2
                        act.wait_ge(half_landed, 16)
                        nc.scalar.activation(whi[:, 0, 0:first], raw[:, 0, 0:first], ACT.Copy).then_inc(half_hi, 1)
                    act.wait_ge(raw_landed[s], 16)
                    nc.scalar.activation(whi[:, s, first:], raw[:, s, first:], ACT.Copy).then_inc(hi_ready, 1)
            act.dma_start(con[:], consts).then_inc(consts_loaded, 16)

            with act.Fori(0, LAYERS) as l:
                def hi(idx, rel, count=None):
                    s = rel % RING
                    act.wait_ge(raw_landed[s], (l * (PIECES // RING) + (idx - s) // RING + 1) * 16
                                if isinstance(idx, int) else count[2])
                    if isinstance(idx, int):
                        old = idx - RING
                        if old < 0:
                            pass
                        elif old in ENDS:
                            act.wait_ge(acc_done, l * TILES + ENDS[old] + 1)
                        else:
                            act.wait_ge(slot_free, l * SLOT_INCS + slot_count(old))
                    elif count[0] == "tile":
                        act.wait_ge(acc_done, count[1])
                    else:
                        act.wait_ge(slot_free, count[1])
                    nc.scalar.activation(whi[:, s, :], raw[:, s, :], ACT.Copy).then_inc(hi_ready, 1)

                def halves(tile, banks):
                    for i, b in enumerate(banks):
                        act.wait_ge(acc_done, l * TILES + tile + i + 1)
                        nc.scalar.activation(half[:, i, :], ps[b][:, S:2 * S], ACT.Copy).then_inc(half_ready, 1)

                def halves_a(g):
                    before = {CV: None, CG: TA[CG], Q0: None, K0: TA[K0], Q1: TA[Q1], K1: TA[K1], PO: TA[K1] + 4}[g]
                    if before:
                        act.wait_ge(evacuated, l * TILES + before + CREDIT)
                    if g == Q0:
                        act.wait_ge(glu_ready, l + 1)
                    halves(TA[g], A_BANKS[g])

                def residual_hi(g, tile, gains):
                    for i in range(NT):
                        c = 4 * g + i
                        act.wait_ge(evacuated, l * TILES + tile + i + 1 + CREDIT)
                        gain_hi(c, gains)

                def rms(n):
                    act.wait_ge(stat_done, l * 2 + n + 1)
                    w = S + 2 if n == 0 else S
                    nc.scalar.activation(rstd[:, 0:w], ps[4][:, 0:w], ACT.Sqrt, bias=eps[:, 0:1],
                                         scale=1.0 / DM).then_inc(rms_ready, 1)

                hooks = {}

                def at(idx, fn, *args):
                    hooks.setdefault(idx, []).append((fn, args))

                def run(a, b):
                    for idx in range(a, b):
                        hi(idx, idx)
                        for fn, args in hooks.get(idx, ()):
                            fn(*args)

                def load_params():
                    act.wait_ge(evacuated, l * TILES + CREDIT)
                    act.wait_ge(xg_ready, l * 32 + KC)
                    act.dma_start(par[:, 0:NPAR], params[bass.ds(l, 1)].rearrange("o p n -> p (o n)")) \
                        .then_inc(params_loaded, 16)

                def load_lam():
                    act.dma_start(lam_in, lamv[bass.ds(l, 1)].partition_broadcast(P)).then_inc(lam_loaded, 16)

                def load_pointwise():
                    act.dma_start(pw_sb[:], pww[bass.ds(l, 1)].rearrange("o p c n -> p (o c) n")) \
                        .then_inc(pointwise_landed, 16)

                def load_poolw():
                    act.dma_start(poolw_sb[:], poolw[bass.ds(l, 1)].rearrange("o p c n -> p (o c) n")) \
                        .then_inc(poolw_landed, 16)

                def lam_exps():
                    act.wait_ge(params_loaded, (l + 1) * 16)
                    act.wait_ge(lam_dots, l + 1)
                    nc.scalar.activation(sm[:, 0, 0:2], mx[:, 0, 0:2], ACT.Exp).then_inc(lam_exp, 1)

                def sigmoid():
                    act.wait_ge(gate_scaled, l + 1)
                    nc.scalar.activation(half[:], half[:], ACT.Sigmoid).then_inc(gated, 1)

                def ln_mean():
                    act.wait_ge(lnsum_done, l + 1)
                    nc.scalar.activation(y[:, 0, :], MISC, ACT.Copy, scale=1.0 / (4 * P)).then_inc(mean_ready, 1)

                def ln_square():
                    act.wait_ge(centred, l + 1)
                    nc.scalar.activation(y[:], gt[:, :, 0:S], ACT.Square).then_inc(squared, 1)

                def ln_std():
                    act.wait_ge(lnsq_done, l + 1)
                    nc.scalar.activation(y[:, 0, :], MISC, ACT.Sqrt, bias=eps[:, 1:2],
                                         scale=1.0 / (4 * P)).then_inc(lnstd_ready, 1)

                def swish():
                    act.wait_ge(normed, l + 1)
                    for i in range(4):
                        nc.scalar.activation(gt[:, i, 0:S], gt[:, i, 0:S], ACT.Silu, bias=par[:, P_LB + i:P_LB + i + 1],
                                             scale=par[:, P_LG + i:P_LG + i + 1]).then_inc(swish_ready, 1)

                def pw_hi(i):
                    act.wait_ge(pw_done, l * 4 + i + 1)
                    nc.scalar.activation(mix[:, 12 + i, 0:S], MISC, ACT.Identity,
                                         bias=par[:, P_PB + i:P_PB + i + 1]).then_inc(chi_ready, 1)

                def exps(h):
                    act.wait_ge(max_ready, l * NH + h + 1)
                    for b in range(2):
                        for m in range(2):
                            e = E[:, h % 2, m, b * P:P + 2 * P * b]
                            nc.scalar.activation(e, e, ACT.Exp, bias=nmx[:, h, 2 * b + m:2 * b + m + 1],
                                                 accum_out=sm[:, h, 2 * b + m:2 * b + m + 1]).then_inc(exp_ready, 1)

                def scale_first(h):
                    act.wait_ge(norms_ready, l * NH + h + 1)
                    if h:
                        act.wait_ge(attT_done, l * NH + h)
                    for b in range(2):
                        nc.scalar.activation(att[:, b * P:P + 2 * P * b], E[:, h % 2, 0, b * P:P + 2 * P * b], ACT.Copy,
                                             scale=rs[:, h, 2 * b:2 * b + 1]).then_inc(first_map, 1)

                def copy_attT(h):
                    act.wait_ge(attT_done, l * NH + h + 1)
                    if h:
                        act.wait_ge(head_done, l * NH + h)
                    nc.scalar.activation(attT[:], AT[:, 0:3 * P], ACT.Copy).then_inc(attT_ready, 1)

                def head_squares(h):
                    act.wait_ge(head_copied, l * NH + h + 1)
                    if h:
                        act.wait_ge(head_sq, l * 16 + 2 * h)
                    for b in range(2):
                        nc.scalar.activation(junk[:, b, :], OUT[:, b * P:b * P + P], ACT.Square,
                                             accum_out=hs[:, h, b:b + 1]).then_inc(head_sq, 1)

                def heads_rms(q):
                    act.wait_ge(head_sq, l * 16 + 8 * q + 8)
                    nc.scalar.activation(hr[:, 4 * q:4 * q + 4, :], hs[:, 4 * q:4 * q + 4, :], ACT.Sqrt,
                                         bias=eps[:, 0:1], scale=1.0 / P).then_inc(head_rms, 1)

                def head_hi(h, region):
                    act.wait_ge(headT_done, l * NH + h + 1)
                    nc.scalar.activation(mix[:, h, 0:S], region, ACT.Copy,
                                         scale=par[:, P_HG + h:P_HG + h + 1]).then_inc(hhi_ready, 1)

                def pool_hi(*tiles):
                    for i in tiles:
                        act.wait_ge(pool_done, l * 4 + i + 1)
                        nc.scalar.activation(mix[:, 8 + i, 0:S], POOLED[i], ACT.Copy,
                                             scale=par[:, P_PS + i:P_PS + i + 1]).then_inc(phi_ready, 1)

                def gate_halves(j, tile, nt):
                    if isinstance(j, int) and j == 0:
                        act.wait_ge(evacuated, l * TILES + TC + CREDIT)
                    else:
                        act.wait_ge(hidden_ready, l * FFG + j)
                    halves(tile, range(nt))

                def gate_taps(j, nt):
                    act.wait_ge(gate_ready, l * FFG + j + 1)
                    for i in range(nt):
                        col = P_FF + (j * NT + i) * 4
                        nc.scalar.activation(y[:, i, :], gt[:, i, 2:S + 2], ACT.Identity,
                                             bias=par[:, bass.ds(col + 3, 1)],
                                             scale=par[:, bass.ds(col + 2, 1)]).then_inc(tap_ready, 1)

                def gate_silu(j, nt):
                    act.wait_ge(taps_done, l * FC + j * NT + nt)
                    nc.scalar.activation(y[:, 0:nt, :], y[:, 0:nt, :], ACT.Silu).then_inc(silu_ready, 1)

                def up_halves(j, tile, nt):
                    act.wait_ge(evacuated, l * TILES + tile + CREDIT)
                    halves(tile, [4 + i for i in range(nt)])

                def hidden_hi(j, nt):
                    act.wait_ge(hid_ready, l * FFG + j + 1)
                    nc.scalar.activation(hidden[:, bass.ds(j * NT, nt), 0:S], half[:, 0:nt, :],
                                         ACT.Copy).then_inc(hidhi_ready, 1)

                for idx, load in ((6, load_params), (7, load_lam), (10, load_pointwise), (12, load_poolw)):
                    at(idx, load)
                at(8, rms, 0)
                at(13, lam_exps)
                for i in range(4):
                    at(LN_AT + 14 + i, pw_hi, i)
                for h in range(NH):
                    n = SCORE_AT[h]
                    at(n + 4, exps, h)
                    at(n + 6, scale_first, h)
                    at(n + 8, copy_attT, h)
                    at(VALUES_AT[h] + 3, head_squares, h)
                at(63, heads_rms, 0)
                at(VALUES_AT[7] + 4, heads_rms, 1)
                at(18, sigmoid)
                at(LN_AT + 3, ln_mean)
                at(LN_AT + 5, ln_square)
                at(LN_AT + 9, ln_std)
                at(LN_AT + 11, swish)
                for h in range(4):
                    at(68 + 2 * h, head_hi, h, MISC)
                    at(79 + h // 2, head_hi, 4 + h, HEADS[h])
                at(77, pool_hi, 0, 1)
                at(78, pool_hi, 2, 3)
                for g in range(9):
                    if g not in (V0, V1):
                        at(8 * g + 9, halves_a, g)
                for g in range(4):
                    at(B0 + 8 * g + 10, residual_hi, g, TB + 4 * g, P_NF)
                at(C0 + 8, rms, 1)

                def pair_hooks(put, j, c, tile, ng, nt):
                    put(c + ng + 2, gate_halves, j, tile, nt)
                    put(c + ng + 3, gate_taps, j, nt)
                    put(c + ng + 5, gate_silu, j, nt)
                    put(c + 2 * ng + 2, up_halves, j, tile + NT, nt)
                    put(c + 2 * ng + 4, hidden_hi, j, nt)

                pair_hooks(at, 0, C0, TC, 8, NT)
                pair_hooks(at, CJ, CT, TT, 6, CR)
                for g in range(2):
                    at(D0 + DP * (g + 1) + 2, residual_hi, g, TD + 4 * g, P_NN)
                act.wait_ge(evacuated, l * TILES + CREDIT - 3)
                hi(2, 2)
                act.wait_ge(evacuated, l * TILES + CREDIT)
                hi(3, 3)
                act.wait_ge(x_loaded[X_LOADS[8]], 16)
                for c in range(FIRST_X, 12):
                    gain_hi(c, P_NN)
                act.wait_ge(x_loaded[X_LOADS[12]], 16)
                for i in range(NT):
                    act.wait_ge(evacuated, l * TILES + CREDIT - 3 + i)
                    square(i)
                run(4, 5)
                for c in range(12, KC):
                    gain_hi(c, P_NN)
                run(5, C0 + 21)
                with act.Fori(1, CJ) as j:
                    own = {}
                    pair_hooks(lambda k, *f: own.setdefault(k, []).append(f), j, 0, j * 8 + TC, 8, NT)
                    for rel in range(5, 21):
                        old = C0 + rel - RING
                        count = (("tile", l * TILES + j * 8 + ENDS[old] + 1) if old in ENDS else
                                 ("slot", l * SLOT_INCS + j * 14 + slot_count(old)))
                        s = (C0 + rel) % RING
                        landed = (l * (PIECES // RING) + j * 4 + (C0 + rel - s) // RING + 1) * 16
                        hi(j, C0 + rel, count=count + (landed,))
                        for f in own.get(rel, ()):
                            f[0](*f[1:])
                run(CT + 5, PIECES + 2)

            nc.scalar.activation(credit[:, 0:1], eps[:, 0:1], ACT.Sqrt)
            for i in range(NT):
                act.wait_ge(evacuated, LAYERS * TILES + CREDIT - 3 + i)
                square(i)
            act.wait_ge(stat_done, 2 * LAYERS + 1)
            nc.scalar.activation(rstd[:, 0:S], ps[0][:, 0:S], ACT.Sqrt, bias=eps[:, 0:1],
                                 scale=1.0 / DM).then_inc(rms_ready, 1)
            act.wait_ge(ssq_part, LAYERS + 1)
            act.wait_ge(xg_ready, 32 * LAYERS + POOL_CHUNKS)
            for c in range(POOL_CHUNKS):
                nc.scalar.activation(x[:, c, :], x[:, c, :], ACT.Copy,
                                     scale=par[:, P_NN + c:P_NN + c + 1]).then_inc(prescaled, 1)

        @block.vector
        def _(dve):
            st = Steps(dve, dve_step)
            step, settle = st.step, st.settle
            step(nc.vector.memset(eps[:, 0:1], 1e-6))
            step(nc.vector.memset(eps[:, 1:2], 1e-5))
            nc.vector.memset(credit[:, 1:2], 0.0).then_inc(evacuated, CREDIT)
            def gain_lo(c, gains, count):
                dve.wait_ge(xhi_ready, count)
                nc.vector.scalar_tensor_tensor(out=xg[:, c, S:2 * S], in0=x[:, c, :],
                                               scalar=par[:, gains + c:gains + c + 1], in1=xg[:, c, 0:S],
                                               op0=ALU.mult, op1=ALU.subtract).then_inc(xg_ready, 1)

            dve.wait_ge(gain_loaded, 16)
            for c in range(FIRST_X):
                gain_lo(c, P_NN, c + 1)
                if c in (1, 3):
                    s, first = c // 2, 0
                    if s == 0:
                        first = PIECE // 2
                        dve.wait_ge(half_hi, 1)
                        nc.vector.tensor_tensor(wlo[:, 0, 0:first], raw[:, 0, 0:first], whi[:, 0, 0:first], ALU.subtract)
                    dve.wait_ge(hi_ready, s + 1)
                    nc.vector.tensor_tensor(wlo[:, s, first:], raw[:, s, first:], whi[:, s, first:],
                                            ALU.subtract).then_inc(lo_ready, 1)
            START = st.n

            with dve.Fori(0, LAYERS) as l:
                st.rebase(l * DVE_STEPS + START)

                def lo(idx, rel):
                    s = rel % RING
                    dve.wait_ge(hi_ready, l * PIECES + idx + 1)
                    nc.vector.tensor_tensor(wlo[:, s, :], raw[:, s, :], whi[:, s, :], ALU.subtract).then_inc(lo_ready, 1)

                def add_halves(tile, banks, dst, h0):
                    for i, b in enumerate(banks):
                        dve.wait_ge(half_ready, l * HALVES + h0 + i + 1)
                        nc.vector.tensor_tensor(dst[i], ps[b][:, 0:S], half[:, i, :], ALU.add) \
                            .then_inc(evacuated, 1 if i < len(banks) - 1 else NT - i)
                    dve.wait_ge(evacuated, l * TILES + tile + NT + CREDIT)

                def rbc(nt):
                    return rstd[:, None, 0:S].to_broadcast([P, nt, S])

                H0 = {CV: 0, CG: 4, Q0: 8, K0: 12, Q1: 16, K1: 20, PO: 24}

                def evac_c(g):
                    dst = [glu[:, i, PAD:] for i in range(NT)] if g == CV else [half[:, i, :] for i in range(NT)]
                    if g == CV:
                        dve.wait_ge(acc_done, l * TILES + 1)
                        step(nc.vector.memset(glu[:, :, 0:PAD], 0.0))
                        dve.wait_ge(rstd_ready, l * 2 + 1)
                    add_halves(TA[g], A_BANKS[g], dst, H0[g])
                    if g == CV:
                        step(nc.vector.tensor_tensor(glu[:, :, PAD:], glu[:, :, PAD:], rbc(NT), ALU.mult))
                    else:
                        nc.vector.tensor_tensor(half[:], half[:], rbc(NT), ALU.mult).then_inc(gate_scaled, 1)

                def make_glu():
                    dve.wait_ge(gated, l + 1)
                    settle()
                    nc.vector.tensor_tensor(glu[:, :, PAD:], glu[:, :, PAD:], half[:], ALU.mult).then_inc(glu_ready, 1)

                taps = [(k, i) for k in range(CONV_K) for i in range(2)]

                def conv(a, b):
                    for n in range(a, min(b, len(taps))):
                        k, i = taps[n]
                        w = par[:, P_DW + i * CONV_K + k:P_DW + i * CONV_K + k + 1]
                        if k == 0:
                            if n == 0:
                                dve.wait_ge(glu_ready, l + 1)
                            step(nc.vector.tensor_scalar(gt[:, i, 0:S], glu[:, i, 0:S], w,
                                                         par[:, P_DB + i:P_DB + i + 1], ALU.mult, ALU.add))
                            continue
                        settle(1 - (i if k == CONV_K - 1 else 0))
                        ins = nc.vector.scalar_tensor_tensor(out=gt[:, i, 0:S], in0=glu[:, i, k:k + S], scalar=w,
                                                             in1=gt[:, i, 0:S], op0=ALU.mult, op1=ALU.add)
                        if k == CONV_K - 1:
                            ins.then_inc(conv_done, 1)
                        else:
                            step(ins)

                def ln_centre():
                    dve.wait_ge(mean_ready, l + 1)
                    nc.vector.tensor_tensor(gt[:, :, 0:S], gt[:, :, 0:S], y[:, 0:1, :].to_broadcast([P, NT, S]),
                                            ALU.subtract).then_inc(centred, 1)

                def ln_scale():
                    dve.wait_ge(lnstd_ready, l + 1)
                    step(nc.vector.reciprocal(y[:, 1, :], y[:, 0, :]))
                    settle()
                    nc.vector.tensor_tensor(gt[:, :, 0:S], gt[:, :, 0:S], y[:, 1:2, :].to_broadcast([P, NT, S]),
                                            ALU.mult).then_inc(normed, 1)

                def pw_lo(i):
                    dve.wait_ge(chi_ready, l * 4 + i + 1)
                    nc.vector.scalar_tensor_tensor(out=mix[:, 12 + i, S:2 * S], in0=MISC,
                                                   scalar=par[:, P_PB + i:P_PB + i + 1], in1=mix[:, 12 + i, 0:S],
                                                   op0=ALU.add, op1=ALU.subtract).then_inc(mixc_ready, 1)

                def evac_v(g):
                    hd = 0 if g == V0 else 4 * P
                    for t in range(2):
                        dve.wait_ge(acc_done, l * TILES + TA[g] + t + 1)
                        nc.vector.tensor_scalar(v[:, t, hd:hd + 4 * P], ps[A_BANKS[g][t]][:], rstd[:, S + t:S + t + 1], None,
                                                ALU.mult).then_inc(evacuated, 1)

                def evac_qk(g):
                    t, h = (qT, kT)[g in (K0, K1)], (0 if g in (Q0, K0) else 4)
                    add_halves(TA[g], A_BANKS[g], [t[:, h + i, :] for i in range(NT)], H0[g])
                    scale = HALF ** -0.5 if t is qT else 1.0
                    nc.vector.scalar_tensor_tensor(out=t[:, h:h + 4, :], in0=t[:, h:h + 4, :], scalar=scale,
                                                   in1=rbc(NT), op0=ALU.mult, op1=ALU.mult).then_inc(qkv_ready, 1)

                def maxes(h):
                    dve.wait_ge(bias_ready, l * NH + h + 1)
                    dve.wait_ge(scores_done, l * NH + h + 1)
                    step(nc.vector.memset(nmx[:, h, :], 0.0))
                    for b in range(2):
                        for m, bank in enumerate((S0, S1)):
                            sl = slice(b * P, P + 2 * P * b)
                            step(nc.vector.tensor_tensor_reduce(
                                out=E[:, h % 2, m, sl], in0=bank[:, sl], in1=bias[:, h % 2, P * (1 - b):S], scale=1.0,
                                scalar=-3.0e38, op0=ALU.add, op1=ALU.max, accum_out=mx[:, h, 2 * b + m:2 * b + m + 1]))
                    settle()
                    nc.vector.tensor_scalar(nmx[:, h, :], mx[:, h, :], -1.0, None, ALU.mult).then_inc(max_ready, 1)

                def inverse_sums(h):
                    dve.wait_ge(exp_ready, l * 32 + 4 * h + 4)
                    step(nc.vector.reciprocal(rs[:, h, :], sm[:, h, :]))
                    settle()
                    r2 = rs[:, h, :].rearrange("p (b m) -> p b m", m=2)[:, :, 1]
                    nc.vector.tensor_scalar(r2, r2, par[:, P_LAM:P_LAM + 1], None, ALU.mult).then_inc(norms_ready, 1)

                def combine(h):
                    for b in range(2):
                        dve.wait_ge(first_map, l * 16 + 2 * h + b + 1)
                        sl = slice(b * P, P + 2 * P * b)
                        nc.vector.scalar_tensor_tensor(out=att[:, sl], in0=E[:, h % 2, 1, sl],
                                                       scalar=rs[:, h, 2 * b + 1:2 * b + 2], in1=att[:, sl],
                                                       op0=ALU.mult, op1=ALU.add).then_inc(att_ready, 1)

                def copy_head(h):
                    dve.wait_ge(head_done, l * NH + h + 1)
                    nc.vector.tensor_copy(qT[:, h, :], OUT).then_inc(head_copied, 1)

                def scale_heads(q):
                    dve.wait_ge(head_rms, l * 2 + q + 1)
                    step(nc.vector.reciprocal(hr[:, 4 * q:4 * q + 4, :], hr[:, 4 * q:4 * q + 4, :]))
                    settle()
                    dve.wait_ge(head_copied, l * NH + 4 * q + 4)
                    for h in range(4 * q, 4 * q + 4):
                        for b in range(2):
                            o = qT[:, h, b * P:b * P + P]
                            nc.vector.tensor_scalar(o, o, hr[:, h, b:b + 1], None, ALU.mult).then_inc(head_scaled, 1)

                def head_lo(h, region):
                    dve.wait_ge(hhi_ready, l * NH + h + 1)
                    nc.vector.scalar_tensor_tensor(out=mix[:, h, S:2 * S], in0=region,
                                                   scalar=par[:, P_HG + h:P_HG + h + 1], in1=mix[:, h, 0:S],
                                                   op0=ALU.mult, op1=ALU.subtract).then_inc(mixh_ready, 1)

                def evac_pool():
                    add_halves(TA[PO], A_BANKS[PO], [glu[:, i, PAD:] for i in range(NT)], H0[PO])
                    nc.vector.tensor_tensor(glu[:, :, PAD:], glu[:, :, PAD:], rbc(NT), ALU.mult).then_inc(pool_in, 1)
                    dve.wait_ge(pool_in, l + 1)

                W = PAD + S
                yw = y[:].rearrange("p a b -> p (a b)")
                sums2 = yw[:, 0:2 * W].rearrange("p (i w) -> p i w", i=2)
                sums4 = yw[:, 2 * W:3 * W]

                def windows():
                    step(nc.vector.tensor_tensor(sums2[:, :, 1:W], glu[:, 0:2, 1:W], glu[:, 0:2, 0:W - 1], ALU.add))
                    settle()
                    step(nc.vector.tensor_tensor(sums4[:, 3:W], sums2[:, 1, 3:W], sums2[:, 1, 1:W - 2], ALU.add))
                    settle()

                def pooled(*pairs):
                    if pairs[0][0] == 2:
                        dve.wait_ge(windowed, l + 1)
                    for i, src in pairs:
                        step(nc.vector.tensor_tensor(half[:, i, 0:16], src[:, PAD:PAD + 16],
                                                     con[:, K_IC + 16 * i:K_IC + 16 * i + 16], ALU.mult))
                        nc.vector.scalar_tensor_tensor(out=half[:, i, 16:S], in0=src[:, PAD + 16:W],
                                                       scalar=1.0 / POOL_WINDOWS[i], in1=glu[:, i, PAD + 16:W],
                                                       op0=ALU.mult, op1=ALU.subtract).then_inc(pooled_ready, 1)
                    settle()
                    i = pairs[0][0]
                    nc.vector.tensor_tensor(half[:, i:i + 2, 0:16], half[:, i:i + 2, 0:16], glu[:, i:i + 2, PAD:PAD + 16],
                                            ALU.subtract).then_inc(pooled_ready, 1)

                def pool_lo(*tiles):
                    for i in tiles:
                        dve.wait_ge(phi_ready, l * 4 + i + 1)
                        nc.vector.scalar_tensor_tensor(out=mix[:, 8 + i, S:2 * S], in0=POOLED[i],
                                                       scalar=par[:, P_PS + i:P_PS + i + 1], in1=mix[:, 8 + i, 0:S],
                                                       op0=ALU.mult, op1=ALU.subtract).then_inc(mixp_ready, 1)

                def lam_products():
                    dve.wait_ge(lam_loaded, (l + 1) * 16)
                    for m in range(2):
                        step(nc.vector.tensor_tensor(lam_prod[:, 64 * m:64 * m + 64], lam_in[:, 128 * m:128 * m + 64],
                                                     lam_in[:, 128 * m + 64:128 * m + 128], ALU.mult))
                    settle()
                    nc.vector.tensor_reduce(mx[:, 0, 0:2], lam_prod.rearrange("p (m d) -> p m d", m=2),
                                            AX.X, ALU.add).then_inc(lam_dots, 1)

                def lam_and_gains():
                    dve.wait_ge(lam_exp, l + 1)
                    dve.wait_ge(params_loaded, (l + 1) * 16)
                    step(nc.vector.tensor_tensor(par[:, P_LAM:P_LAM + 1], sm[:, 0, 1:2], sm[:, 0, 0:1], ALU.subtract))
                    step(nc.vector.tensor_scalar(par[:, P_HG:P_HG + NH], par[:, P_HG:P_HG + NH],
                                                 par[:, P_LI + 1:P_LI + 2], None, ALU.mult))
                    settle()
                    step(nc.vector.tensor_tensor(par[:, P_LAM:P_LAM + 1], par[:, P_LAM:P_LAM + 1],
                                                 par[:, P_LI:P_LI + 1], ALU.add))
                    settle()

                def inverse_rms(n):
                    dve.wait_ge(rms_ready, l * 2 + n + 1)
                    w = S + 2 if n == 0 else S
                    nc.vector.reciprocal(rstd[:, 0:w], rstd[:, 0:w]).then_inc(rstd_ready, 1)
                    dve.wait_ge(rstd_ready, l * 2 + n + 1)

                def residual_sums(g, tile, banks):
                    for i, b in enumerate(banks):
                        dve.wait_ge(acc_done, l * TILES + tile + i + 1)
                        step(nc.vector.tensor_tensor(half[:, i, :], ps[b][:, 0:S], x[:, 4 * g + i, :], ALU.add))
                    for i, b in enumerate(banks):
                        settle(3 - i)
                        nc.vector.tensor_tensor(x[:, 4 * g + i, :], ps[b][:, S:2 * S], half[:, i, :],
                                                ALU.add).then_inc(evacuated, 1)

                def residual(g, tile, first, gains, banks):
                    residual_sums(g, tile, banks)
                    if gains == P_NN and g >= FIRST_X // NT:
                        return
                    for c in range(4 * g, 4 * g + NT):
                        gain_lo(c, gains, l * 32 + KC + first + c + 1)

                def gate_sums(j, tile, h0, nt):
                    add_halves(tile, range(nt), [gt[:, i, 2:] for i in range(nt)], h0)
                    nc.vector.tensor_tensor(gt[:, 0:nt, 2:], gt[:, 0:nt, 2:], rbc(nt), ALU.mult).then_inc(gate_ready, 1)

                def gate_taps(j, nt):
                    for k in (1, 0):
                        for i in range(nt):
                            col = P_FF + (j * NT + i) * 4 + k
                            if k:
                                dve.wait_ge(tap_ready, l * FC + j * NT + i + 1)
                            else:
                                settle(nt - 1 - i)
                            ins = nc.vector.scalar_tensor_tensor(out=y[:, i, :], in0=gt[:, i, k:k + S],
                                                                 scalar=par[:, bass.ds(col, 1)], in1=y[:, i, :],
                                                                 op0=ALU.mult, op1=ALU.add)
                            if k:
                                step(ins)
                            else:
                                ins.then_inc(taps_done, 1)

                def up_sums(j, tile, h0, nt):
                    add_halves(tile, [4 + i for i in range(nt)], [half[:, i, :] for i in range(nt)], h0)
                    step(nc.vector.tensor_tensor(half[:, 0:nt, :], half[:, 0:nt, :], rbc(nt), ALU.mult))

                def hidden_product(j, nt):
                    dve.wait_ge(silu_ready, l * FFG + j + 1)
                    settle()
                    nc.vector.tensor_tensor(half[:, 0:nt, :], half[:, 0:nt, :], y[:, 0:nt, :], ALU.mult) \
                        .then_inc(hid_ready, 1)

                def hidden_lo(j, nt):
                    dve.wait_ge(hidhi_ready, l * FFG + j + 1)
                    nc.vector.tensor_tensor(hidden[:, bass.ds(j * NT, nt), S:2 * S], half[:, 0:nt, :],
                                            hidden[:, bass.ds(j * NT, nt), 0:S], ALU.subtract).then_inc(hidden_ready, 1)

                def zero_front():
                    step(nc.vector.memset(gt[:, :, 0:2], 0.0))
                    settle()

                hooks = {}

                def at(idx, fn, *args):
                    hooks.setdefault(idx, []).append((fn, args))

                def run(a, b):
                    for idx in range(a, b):
                        lo(idx, idx)
                        for fn, args in hooks.get(idx, ()):
                            fn(*args)

                at(8, inverse_rms, 0)
                at(12, lam_products)
                at(14, lam_and_gains)
                for i in range(4):
                    at(LN_AT + 14 + i, pw_lo, i)
                for h in range(NH):
                    n = SCORE_AT[h]
                    at(n + 3, maxes, h)
                    at(n + 5, inverse_sums, h)
                    at(n + 6, combine, h)
                    at(VALUES_AT[h] + 3, copy_head, h)
                at(64, scale_heads, 0)
                at(18, make_glu)
                at(LN_AT + 4, ln_centre)
                at(LN_AT + 10, ln_scale)
                for h in range(4):
                    at(68 + 2 * h, head_lo, h, MISC)
                    at(79 + h // 2, head_lo, 4 + h, HEADS[h])
                for n in range(31):
                    at(19 + n, conv, 2 * n, 2 * n + 2)
                for g in (CV, CG):
                    at(8 * g + 9, evac_c, g)
                for g in (V0, V1):
                    at(8 * g + 9, evac_v, g)
                for g in (Q0, K0, Q1, K1):
                    at(8 * g + 9, evac_qk, g)
                at(73, evac_pool)
                at(74, windows)
                at(74, pooled, (0, sums2[:, 0, :]), (1, sums4))
                at(76, pool_lo, 0, 1)
                at(76, scale_heads, 1)
                at(75, pooled, (2, win0[:, 0, :]), (3, win1[:, 1, :]))
                at(78, pool_lo, 2, 3)
                for g in range(4):
                    at(B0 + 8 * g + 10, residual, g, TB + 4 * g, 0, P_NF, [4 * (g % 2) + i for i in range(NT)])
                at(C0 + 8, inverse_rms, 1)
                at(C0 + 9, zero_front)

                def pair_hooks(put, j, c, tile, ng, nt):
                    h0 = j * 8 + HC
                    put(c + ng + 2, gate_sums, j, tile, h0, nt)
                    put(c + ng + 4, gate_taps, j, nt)
                    put(c + 2 * ng + 2, up_sums, j, tile + NT, h0 + nt, nt)
                    put(c + 2 * ng + 3, hidden_product, j, nt)
                    put(c + 2 * ng + 4, hidden_lo, j, nt)

                pair_hooks(at, 0, C0, TC, 8, NT)
                pair_hooks(at, CJ, CT, TT, 6, CR)
                for g in range(3):
                    at(D0 + DP * (g + 1) + 2, residual, g, TD + 4 * g, 16, P_NN, [4 * (g % 2) + i for i in range(NT)])
                lo(2, 2)
                lo(3, 3)
                for c in range(FIRST_X, 12):
                    gain_lo(c, P_NN, l * 32 + c + 1)
                run(4, 5)
                for c in range(12, KC):
                    gain_lo(c, P_NN, l * 32 + c + 1)
                run(5, C0 + 21)
                before = st.n
                with dve.Fori(1, CJ) as j:
                    st.rebase(l * DVE_STEPS + START + before + (j - 1) * DVE_LOOP)
                    own = {}
                    pair_hooks(lambda k, *f: own.setdefault(k, []).append(f), j, 0, j * 8 + TC, 8, NT)
                    for rel in range(5, 21):
                        lo(j * 16 + C0 + rel, C0 + rel)
                        for f in own.get(rel, ()):
                            f[0](*f[1:])
                SEEN["loop"] = st.n
                st.rebase(l * DVE_STEPS + START)
                st.n = before + (CJ - 1) * DVE_LOOP
                run(CT + 5, PIECES + 2)
                residual_sums(3, TD + 12, [4 + i for i in range(NT)])
                SEEN["dve"] = st.n
            dve.wait_ge(rms_ready, 2 * LAYERS + 1)
            nc.vector.reciprocal(rstd[:, 0:S], rstd[:, 0:S]).then_inc(rstd_ready, 1)
            dve.wait_ge(rstd_ready, 2 * LAYERS + 1)
            for c in range(POOL_CHUNKS, KC):
                nc.vector.scalar_tensor_tensor(out=x[:, c, :], in0=x[:, c, :], scalar=par[:, P_NN + c:P_NN + c + 1],
                                               in1=rstd[:, 0:S], op0=ALU.mult, op1=ALU.mult).then_inc(final_scaled, 1)

        @block.gpsimd
        def _(pool):
            st = Steps(pool, pool_step)
            step, settle = st.step, st.settle

            def hold_waits():
                settle()
                step(nc.gpsimd.tensor_tensor(held[:, 1:2], held[:, 0:1], held[:, 0:1], ALU.mult))

            step(nc.gpsimd.memset(held[:], 0.0))
            settle()

            def square_sum(chunks, done, wait):
                for c in range(chunks):
                    wait(c)
                    dst = ssq[:] if c == 0 else sq[:, c % 2, :]
                    step(nc.gpsimd.tensor_tensor(dst, x[:, c, :], x[:, c, :], ALU.mult))
                    settle()
                    if 0 < c < chunks - 1:
                        step(nc.gpsimd.tensor_tensor(ssq[:], ssq[:], sq[:, c % 2, :], ALU.add))
                        settle()
                    elif c:
                        nc.gpsimd.tensor_tensor(ssq[:], ssq[:], sq[:, c % 2, :], ALU.add).then_inc(done, 1)

            def wait_load(c):
                if c in X_LOADS:
                    pool.wait_ge(x_loaded[X_LOADS[c]], 16)

            square_sum(12, ssq_part, wait_load)
            pool.wait_ge(consts_loaded, 16)
            START = st.n
            with pool.Fori(0, LAYERS) as l:
                st.rebase(l * POOL_STEPS + START)

                pool.wait_ge(ssq_part, l + 1)
                pool.wait_ge(end_squared, l * 4 + 4)
                step(nc.gpsimd.tensor_tensor(sq[:], y[:, 0:2, :], y[:, 2:4, :], ALU.add))
                settle()
                step(nc.gpsimd.tensor_tensor(ssq[:], ssq[:], sq[:, 0, :], ALU.add))
                settle()
                nc.gpsimd.tensor_tensor(ssq[:], ssq[:], sq[:, 1, :], ALU.add).then_inc(ssq_ready, 1)

                def head_bias(h):
                    if h >= 2:
                        pool.wait_ge(max_ready, l * NH + h - 1)
                    else:
                        pool.wait_ge(acc_done, l * TILES + 1)
                    hold_waits()
                    nc.gpsimd.tensor_scalar(bias[:, h % 2, :], negdist, 2.0 ** (-8.0 * (h + 1) / NH), None,
                                            ALU.mult).then_inc(bias_ready, 1)

                head_bias(0)
                head_bias(1)
                pool.wait_ge(params_loaded, (l + 1) * 16)
                pool.wait_ge(glu_ready, l + 1)
                for k in range(CONV_K):
                    w = par[:, P_DW + 2 * CONV_K + k:P_DW + 3 * CONV_K + k + 1:CONV_K]
                    step(nc.gpsimd.tensor_tensor(sq[:], glu[:, 2:4, k:k + S], w[:, :, None].to_broadcast([P, 2, S]),
                                                 ALU.mult))
                    settle()
                    acc = gt[:, 2:4, 0:S] if k else par[:, P_DB + 2:P_DB + 4][:, :, None].to_broadcast([P, 2, S])
                    ins = nc.gpsimd.tensor_tensor(gt[:, 2:4, 0:S], sq[:], acc, ALU.add)
                    if k < CONV_K - 1:
                        step(ins)
                        settle()
                    else:
                        ins.then_inc(pconv_done, 1)
                head_bias(2)
                head_bias(3)
                pool.wait_ge(conv_done, l * 2 + 2)
                pool.wait_ge(pconv_done, l + 1)
                step(nc.gpsimd.tensor_tensor(sq[:], gt[:, 0:2, 0:S], gt[:, 2:4, 0:S], ALU.add))
                settle()
                nc.gpsimd.tensor_tensor(sq[:, 0, :], sq[:, 0, :], sq[:, 1, :], ALU.add).then_inc(presummed, 1)
                head_bias(4)
                head_bias(5)
                pool.wait_ge(presummed, l * 2 + 1)
                pool.wait_ge(squared, l + 1)
                step(nc.gpsimd.tensor_tensor(sq[:], y[:, 0:2, :], y[:, 2:4, :], ALU.add))
                settle()
                nc.gpsimd.tensor_tensor(sq[:, 0, :], sq[:, 0, :], sq[:, 1, :], ALU.add).then_inc(presummed, 1)
                head_bias(6)
                head_bias(7)
                pool.wait_ge(pool_in, l + 1)
                W = PAD + S
                step(nc.gpsimd.tensor_tensor(win0[:, :, 1:W], glu[:, 2:4, 1:W], glu[:, 2:4, 0:W - 1], ALU.add))
                settle()
                step(nc.gpsimd.tensor_tensor(win1[:, :, 3:W], win0[:, :, 3:W], win0[:, :, 1:W - 2], ALU.add))
                settle()
                step(nc.gpsimd.tensor_tensor(win0[:, :, 7:W], win1[:, :, 7:W], win1[:, :, 3:W - 4], ALU.add))
                settle()
                nc.gpsimd.tensor_tensor(win1[:, 1, 15:W], win0[:, 1, 15:W], win0[:, 1, 7:W - 8],
                                        ALU.add).then_inc(windowed, 1)
                square_sum(KC, ssq_ready, lambda c: pool.wait_ge(evacuated, l * TILES + TB + c + 1 + CREDIT))
                pool.wait_ge(ssq_ready, l * 2 + 2)
                pool.wait_ge(stat_done, l * 2 + 2)
                square_sum(12, ssq_part, lambda c: pool.wait_ge(evacuated, l * TILES + TD + c + 1 + CREDIT))
                SEEN["pool"] = st.n
            pool.wait_ge(prescaled, POOL_CHUNKS)
            pool.wait_ge(rstd_ready, 2 * LAYERS + 1)
            nc.gpsimd.tensor_tensor(x[:, 0:POOL_CHUNKS, :], x[:, 0:POOL_CHUNKS, :],
                                    rstd[:, None, 0:S].to_broadcast([P, POOL_CHUNKS, S]), ALU.mult).then_inc(pool_scaled, 1)

        @block.tensor
        def _(pe):
            with pe.Fori(0, LAYERS) as l:
                def tile_block(bank, s, blk, mov, first, last):
                    nc.tensor.matmul(ps[bank][:], whi[:, s, blk * P:blk * P + P], mov, start=first, stop=False)
                    return nc.tensor.matmul(ps[bank][:, 0:S], wlo[:, s, blk * P:blk * P + P], mov[:, 0:S],
                                            start=False, stop=last)

                hooks = {}

                def at(idx, fn, *args):
                    hooks.setdefault(idx, []).append((fn, args))

                def arrived(idx, j=None):
                    pe.wait_ge(lo_ready, l * PIECES + idx + 1)

                def group(piece0, tile, free, banks, nk, moving, ready=None, rel0=None, hook=True):
                    nt = len(banks)
                    rel0 = piece0 if rel0 is None else rel0
                    blocks = [(k, i) for k in range(nk) for i in range(nt)]
                    npieces = -(-len(blocks) // PB)
                    for p in range(npieces):
                        s = (rel0 + p) % RING
                        arrived(piece0 + p)
                        mine = blocks[PB * p:PB * p + PB]
                        order = list(enumerate(mine))
                        if nt == NT and (p == npieces - 1 or p == 0 and not ready):
                            order.sort(key=lambda o: o[1][::-1])
                        for blk, (k, i) in order:
                            if i == 0 and ready:
                                ready(k)
                            if k == 0:
                                pe.wait_ge(evacuated, l * TILES + free[i] + CREDIT)
                            last = tile_block(banks[i], s, blk, moving(k), k == 0, k == nk - 1)
                            if k == nk - 1:
                                last.then_inc(acc_done, 1 if i < nt - 1 else NT - i)
                            elif blk == order[-1][0]:
                                last.then_inc(slot_free, 1)
                        if hook:
                            for fn, args in hooks.get(piece0 + p, ()):
                                fn(*args)

                def v_group(piece0, tile, free, banks):
                    for p in range(8):
                        s = (piece0 + p) % RING
                        arrived(piece0 + p)
                        order = [(kk, t) for kk in range(2) for t in range(2)]
                        if p == 7:
                            order.sort(key=lambda o: o[1])
                        for n, (kk, t) in enumerate(order):
                            k, bank = 2 * p + kk, ps[banks[t]][:]
                            if k == 0:
                                pe.wait_ge(evacuated, l * TILES + free[t] + CREDIT)
                            xh = xg[:, k, t * P:t * P + P]
                            xl = xg[:, k, S + t * P:S + t * P + P]
                            wh = whi[:, s, kk * 512:kk * 512 + 512]
                            wl = wlo[:, s, kk * 512:kk * 512 + 512]
                            nc.tensor.matmul(bank, xh, wh, start=k == 0, stop=False)
                            nc.tensor.matmul(bank, xh, wl, start=False, stop=False)
                            last = nc.tensor.matmul(bank, xl, wh, start=False, stop=k == KC - 1)
                            if k == KC - 1:
                                last.then_inc(acc_done, 1)
                            elif n == 3:
                                last.then_inc(slot_free, 1)
                        for fn, args in hooks.get(piece0 + p, ()):
                            fn(*args)

                def mm(out, lhsT, rhs, first=True, last=True):
                    return nc.tensor.matmul(out, lhsT, rhs, start=first, stop=last)

                def stats(n):
                    pe.wait_ge(consts_loaded, 16)
                    pe.wait_ge(ssq_ready, l * 2 + n + 1)
                    pe.wait_ge(evacuated, l * TILES + (TC if n else 0) + CREDIT)
                    last = mm(ps[4][:, 0:S], ones, ssq[:])
                    if n == 0:
                        mm(ps[4][:, S:S + 1], ssq[:, 0:P], ones[:, 0:1])
                        last = mm(ps[4][:, S + 1:S + 2], ssq[:, P:S], ones[:, 0:1])
                    last.then_inc(stat_done, 1)

                def ln_sum():
                    pe.wait_ge(presummed, l * 2 + 1)
                    mm(MISC, ones, sq[:, 0, :]).then_inc(lnsum_done, 1)

                def ln_sq():
                    pe.wait_ge(presummed, l * 2 + 2)
                    mm(MISC, ones, sq[:, 0, :]).then_inc(lnsq_done, 1)

                def pointwise(d):
                    if d == 0:
                        pe.wait_ge(pointwise_landed, (l + 1) * 16)
                        pe.wait_ge(swish_ready, l * 4 + 4)
                    else:
                        pe.wait_ge(mixc_ready, l * 4 + d)
                    for c in range(4):
                        last = mm(MISC, pw_sb[:, c, d * P:d * P + P], gt[:, c, 0:S], c == 0, c == 3)
                    last.then_inc(pw_done, 1)

                def scores(h):
                    pe.wait_ge(qkv_ready, l * 4 + (2 if h < 4 else 4))
                    if h == 0:
                        pe.wait_ge(rstd_ready, l * 2 + 1)
                    else:
                        pe.wait_ge(max_ready, l * NH + h)
                    for b in range(2):
                        for m, bank in enumerate((S0, S1)):
                            rows = slice(HALF * m, HALF * m + HALF)
                            last = mm(bank[:, b * P:P + 2 * P * b], qT[rows, h, b * P:b * P + P],
                                      kT[rows, h, 0:P * (b + 1)])
                    last.then_inc(scores_done, 1)

                def transpose_att(h):
                    pe.wait_ge(att_ready, l * 16 + 2 * h + 2)
                    if h:
                        pe.wait_ge(head_sq, l * 16 + 2 * h)
                    for n in range(3):
                        last = nc.tensor.transpose(AT[:, n * P:n * P + P], att[:, n * P:n * P + P], ident)
                    last.then_inc(attT_done, 1)

                def values(h):
                    pe.wait_ge(attT_ready, l * NH + h + 1)
                    if h in (0, 4):
                        pe.wait_ge(evacuated, l * TILES + TA[V0 if h == 0 else V1] + 2 + CREDIT)
                    hd = slice(h * P, h * P + P)
                    mm(OUT[:, 0:P], attT[:, 0:P], v[:, 0, hd])
                    mm(OUT[:, P:S], attT[:, P:2 * P], v[:, 0, hd], True, False)
                    mm(OUT[:, P:S], attT[:, 2 * P:3 * P], v[:, 1, hd], False, True).then_inc(head_done, 1)

                def transpose_head(h, region):
                    pe.wait_ge(head_scaled, l * 16 + 2 * h + 2)
                    if h == 0:
                        pe.wait_ge(mixc_ready, l * 4 + 4)
                    elif h < 4:
                        pe.wait_ge(mixh_ready, l * NH + h)
                    else:
                        pe.wait_ge(mixp_ready, l * 4 + h - 3)
                    for b in range(2):
                        last = nc.tensor.transpose(region[:, b * P:b * P + P], qT[:, h, b * P:b * P + P], ident)
                    last.then_inc(headT_done, 1)

                def pool_products(*tiles):
                    pe.wait_ge(poolw_landed, (l + 1) * 16)
                    for i in tiles:
                        pe.wait_ge(pooled_ready, l * 6 + (3 if i < 2 else 6))
                        if i == 0:
                            pe.wait_ge(max_ready, l * NH + NH)
                        elif i == 2:
                            pe.wait_ge(mixh_ready, l * NH + 4)
                        elif i == 3:
                            pe.wait_ge(head_sq, l * 16 + 16)
                        mm(POOLED[i], poolw_sb[:, i, :], half[:, i, :]).then_inc(pool_done, 1)

                at(5, stats, 0)
                at(LN_AT, ln_sum)
                at(LN_AT + 5, ln_sq)
                for i in range(4):
                    at(LN_AT + 11 + i, pointwise, i)
                for h in range(NH):
                    at(SCORE_AT[h] + 5, transpose_att, h)
                    at(VALUES_AT[h], values, h)
                for h in range(NH):
                    at(SCORE_AT[h], scores, h)
                at(74, pool_products, 0, 1)
                at(75, pool_products, 2, 3)
                for h in range(4):
                    at(65 + 2 * h, transpose_head, h, MISC)
                    at(76 + h // 2, transpose_head, 4 + h, HEADS[h])
                at(C0 + 5, stats, 1)

                def x_moving(k):
                    return xg[:, k, :]

                def x_from(n):
                    return lambda k: pe.wait_ge(xg_ready, l * 32 + 16 * n + k + 1)

                last_tile = {b: b - 8 + 1 for b in range(4)}
                for g in range(9):
                    free = [last_tile[b] for b in A_BANKS[g]]
                    if g in (V0, V1):
                        v_group(8 * g, TA[g], free, A_BANKS[g])
                    else:
                        group(8 * g, TA[g], free, A_BANKS[g], KC, x_moving, x_from(0) if g == 0 else None)
                    for i, b in enumerate(A_BANKS[g]):
                        last_tile[b] = TA[g] + i + 1

                def mix_ready(k):
                    c = B_CHUNKS[k]
                    if c >= 12:
                        pe.wait_ge(mixc_ready, l * 4 + c - 12 + 1)
                    elif c < 8:
                        pe.wait_ge(mixh_ready, l * NH + c + 1)
                    else:
                        pe.wait_ge(mixp_ready, l * 4 + c - 8 + 1)

                for g in range(4):
                    tile = TB + 4 * g
                    free = [TA[PO] + i + 1 if g == 0 else 0 if g == 1 else tile + i + 1 - 8 for i in range(4)]
                    group(B0 + 8 * g, tile, free, [4 * (g % 2) + i for i in range(4)], KC,
                          lambda k: mix[:, B_CHUNKS[k], :], mix_ready if g == 0 else None)

                group(C0, TC, [TC + i + 1 - 8 for i in range(4)], range(4), KC, x_moving,
                      x_from(1))
                pe.wait_ge(rstd_ready, l * 2 + 2)
                group(C0 + 8, TC + 4, [TC + 4 + i + 1 - 8 for i in range(4)], range(4, 8), KC, x_moving)
                with pe.Fori(1, CJ) as j:
                    for u in range(2):
                        tile = TC + 4 * u
                        group(j * 16 + C0 + 8 * u, 0, [j * 8 + (tile + i + 1 - 8) for i in range(4)],
                              range(4 * u, 4 * u + 4), KC, x_moving, rel0=C0 + 8 * u, hook=False)
                for u in range(2):
                    group(CT + 6 * u, 0, [TT - 8 + 4 * u + i + 1 for i in range(CR)], range(4 * u, 4 * u + CR),
                          KC, x_moving)

                with pe.Fori(0, 2) as d:
                    for u in range(2):
                        tile = TD + 4 * u
                        group(d * (2 * DP) + D0 + DP * u, 0, [d * 8 + (tile + i + 1 - 8) for i in range(4)],
                              range(4 * u, 4 * u + 4), FC, lambda k: hidden[:, k, :],
                              (lambda k: pe.wait_ge(hidden_ready, l * FFG + k // NT + 1) if k % NT == 0 else None)
                              if u == 0 else None, rel0=D0 + DP * u, hook=False)
            pe.wait_ge(ssq_part, LAYERS + 1)
            pe.wait_ge(evacuated, LAYERS * TILES - NT + CREDIT)
            mm(ps[0][:, 0:S], ones, ssq[:], True, False)
            for i in range(NT):
                pe.wait_ge(end_squared, 4 * LAYERS + i + 1)
                last = mm(ps[0][:, 0:S], ones, y[:, i, :], False, i == NT - 1)
            last.then_inc(stat_done, 1)

    assert SEEN == STEPS, SEEN


def lay_out(a):
    import numpy as np
    f = np.float32
    xT = np.ascontiguousarray(a["x"][0].T.reshape(KC, P, S).transpose(1, 0, 2))

    def blocks(w, cols, chunks):
        nt = cols[1] // P
        n = len(chunks) * nt
        out = np.zeros((-(-n // PB), PB, P, P), f)
        b = w.reshape(-1, P, w.shape[1])[chunks][:, :, cols[0]:cols[0] + cols[1]]
        out.reshape(-1, P, P)[:n] = b.reshape(len(chunks), P, nt, P).transpose(0, 2, 1, 3).reshape(n, P, P)
        return out.transpose(0, 2, 1, 3).reshape(-1, P, PIECE)

    stream = []
    for l in range(LAYERS):
        every = list(range(KC))
        for c in A_COLS:
            stream.append(blocks(a["w_in"][l], (c, 512), every))
        for g in range(4):
            stream.append(blocks(a["w_out"][l], (512 * g, 512), list(B_CHUNKS)))
        for j in range(CJ + 1):
            n = 512 if j < CJ else CR * P
            for u in range(2):
                stream.append(blocks(a["w_ffn_in"][l], (u * FF + 512 * j, n), every))
        for g in range(4):
            stream.append(blocks(a["w_ffn_out"][l], (512 * g, 512), list(range(FC))))
    stream.append(np.zeros((2, P, PIECE), f))
    wstream = np.concatenate(stream)

    def col(v):
        return v.reshape(-1, P).T

    params = np.zeros((LAYERS + 1, P, NPAR), f)
    for l in range(LAYERS):
        q = params[l]
        q[:, P_NF:P_NF + KC] = col(a["norm_ffn"][l])
        q[:, P_NN:P_NN + KC] = col(a["norm_mix"][l + 1] if l + 1 < LAYERS else a["final_norm"])
        q[:, P_HG:P_HG + NH] = a["diff_head_gain"][l].T
        q[:, P_PS:P_PS + 4] = col(a["pool_scale"][l])
        q[:, P_DW:P_DB] = a["conv_dw_w"][l].T.reshape(4, P, CONV_K).transpose(1, 0, 2).reshape(P, -1)
        q[:, P_DB:P_DB + 4] = col(a["conv_dw_b"][l])
        q[:, P_LG:P_LG + 4] = col(a["conv_ln_g"][l])
        q[:, P_LB:P_LB + 4] = col(a["conv_ln_b"][l])
        q[:, P_PB:P_PB + 4] = col(a["conv_pw_b"][l])
        ff = np.concatenate([a["ffn_conv_w"][l], a["ffn_conv_b"][l][None]])
        q[:, P_LI:] = [-lam_init(l), 1 - lam_init(l)]
        q[:, P_FF:P_LI] = ff.T.reshape(FC, P, 4).transpose(1, 0, 2).reshape(P, -1)
    params[LAYERS, :, 0:KC] = col(a["norm_mix"][0])
    lamv = np.stack([a["lam_q1"], a["lam_k1"], a["lam_q2"], a["lam_k2"]], 1).reshape(LAYERS, -1)

    consts = np.zeros((P, NCON), f)
    q, k = P + np.arange(P)[:, None], np.arange(S)[None]
    consts[:, K_ND:K_ND + S] = np.where(k // CHUNK <= q // CHUNK, -np.abs(q - k), -1e30)
    consts[:, K_ID:K_ID + P] = np.eye(P)
    consts[:, K_ON:K_ON + P] = 1
    for i, w in enumerate(POOL_WINDOWS):
        consts[:, K_IC + 16 * i:K_IC + 16 * i + 16] = 1.0 / np.minimum(np.arange(16) + 1, w)
    poolw = np.ascontiguousarray(a["pool_w"].transpose(0, 2, 1, 3))
    pww = np.ascontiguousarray(a["conv_pw_w"].reshape(LAYERS, 4, P, 4 * P).transpose(0, 2, 1, 3))
    return dict(xT=xT, wstream=wstream, params=params, lamv=np.ascontiguousarray(lamv), consts=consts,
                poolw=poolw, pww=pww)


def kernel(**inputs):
    import numpy as np
    import concourse.bacc as bacc
    from concourse import mybir
    from concourse.bass_utils import run_bass_kernel_spmd

    arrays = lay_out({n: np.asarray(v) for n, v in inputs.items()})
    nc = bacc.Bacc("TRN2", target_bir_lowering=False, num_devices=1)
    aps = [nc.dram_tensor(n, v.shape, mybir.dt.from_np(v.dtype), kind="ExternalInput").ap() for n, v in arrays.items()]
    outT = nc.dram_tensor("outT", (P, KC, S), mybir.dt.float32, kind="ExternalOutput").ap()
    program(nc, *aps, outT)
    got = run_bass_kernel_spmd(nc, [arrays], core_ids=[0]).results[0]["outT"]
    return np.ascontiguousarray(got.transpose(2, 1, 0).reshape(1, S, DM))
```
